# Optimizing a Trainium2 kernel written in Bass

```python
import jax, jax.numpy as jnp
from jax import lax
import numpy as np

D_MODEL = 2048
BATCH = 1
SEQ = 512
DEPTH = 1

N_MLA_HEADS = D_MODEL // 256
MLA_NOPE_DIM = 128
ROPE_DIM = 64
MLA_QK_DIM = MLA_NOPE_DIM + ROPE_DIM
MLA_V_DIM = 128
Q_LORA = D_MODEL // 4
KV_LORA = D_MODEL // 8
ROPE_THETA = 10000.0
Q_BLOCK = 128
MLA_WIDTH = N_MLA_HEADS * MLA_V_DIM

N_MLSTM_HEADS = 4
MLSTM_HEAD_DIM = D_MODEL // 8
MLSTM_WIDTH = N_MLSTM_HEADS * MLSTM_HEAD_DIM
MLSTM_CHUNK = 128
CONV_WIDTH = 5
N_GATE_COLS = 4 * N_MLSTM_HEADS

D_MIX = MLA_WIDTH + MLSTM_WIDTH
D_FF = 4 * D_MODEL
IN_SIZES = (Q_LORA, KV_LORA, ROPE_DIM, MLSTM_WIDTH, MLSTM_WIDTH, MLSTM_WIDTH, MLSTM_WIDTH, N_GATE_COLS)
D_IN = sum(IN_SIZES)
IN_SPLIT_POINTS = tuple(int(v) for v in np.cumsum(IN_SIZES)[:-1])
EPS = 1e-6
M_INIT = -1e30

kernel_name = "hybrid_mla_mlstm_adaln_block"

def rmsnorm(x, g):
    xf = x.astype(jnp.float32)
    y = xf * lax.rsqrt(jnp.mean(xf * xf, axis=-1, keepdims=True) + EPS)
    return (y * g.astype(jnp.float32)).astype(x.dtype)

def modulate(h, shift, scale):
    return h * (1 + scale) + shift

def rope(xp, positions):
    half = ROPE_DIM // 2
    freqs = ROPE_THETA ** (-jnp.arange(half, dtype=jnp.float32) / half)
    ang = positions.astype(jnp.float32)[..., None] * freqs
    cos = jnp.cos(ang)[:, :, None, :]
    sin = jnp.sin(ang)[:, :, None, :]
    x1 = xp[..., :half].astype(jnp.float32)
    x2 = xp[..., half:].astype(jnp.float32)
    out = jnp.concatenate([x1 * cos - x2 * sin, x1 * sin + x2 * cos], axis=-1)
    return out.astype(xp.dtype)

def dense_attention_blocks(q, k, v):
    B, S, H, Dq = q.shape
    nb = S // Q_BLOCK
    qb = q.reshape(B, nb, Q_BLOCK, H, Dq).transpose(1, 0, 2, 3, 4)
    scale = Dq ** -0.5

    def one_block(qi):
        s = jnp.einsum('bqhd,bkhd->bhqk', qi, k).astype(jnp.float32) * scale
        p = jax.nn.softmax(s, axis=-1).astype(v.dtype)
        return jnp.einsum('bhqk,bkhd->bqhd', p, v)

    o = lax.map(one_block, qb)
    return o.transpose(1, 0, 2, 3, 4).reshape(B, S, H * v.shape[-1])

def mlstm_chunkwise(q, k, v, log_i, log_f):
    B, H, S, d = q.shape
    L = MLSTM_CHUNK
    nc = S // L
    chunk = lambda t: t.reshape(B, H, nc, L, *t.shape[3:]).swapaxes(0, 2).swapaxes(1, 2)
    qc, kc, vc = chunk(q), chunk(k), chunk(v)
    ic, fc = chunk(log_i), chunk(log_f)
    tril = jnp.tril(jnp.ones((L, L), dtype=bool))

    def step(carry, inp):
        C, n, m = carry
        qt, kt, vt, it, ft = inp
        b = jnp.cumsum(ft, axis=-1)
        log_inter = b + m[..., None]
        logD = jnp.where(tril, b[..., :, None] - b[..., None, :] + it[..., None, :], -jnp.inf)
        m_t = jnp.maximum(log_inter, jnp.max(logD, axis=-1))
        Dm = jnp.exp(logD - m_t[..., None])
        w_inter = jnp.exp(log_inter - m_t)
        scores = jnp.einsum('bhtd,bhsd->bhts', qt, kt) * Dm
        num = jnp.einsum('bhts,bhsd->bhtd', scores, vt) \
            + w_inter[..., None] * jnp.einsum('bhvk,bhtk->bhtv', C, qt)
        den = jnp.sum(scores, axis=-1) + w_inter * jnp.einsum('bhtk,bhk->bht', qt, n)
        h = num / jnp.maximum(jnp.abs(den), jnp.exp(-m_t))[..., None]
        bL = b[..., -1]
        log_w = bL[..., None] - b + it
        m_new = jnp.maximum(bL + m, jnp.max(log_w, axis=-1))
        decay = jnp.exp(bL + m - m_new)
        w = jnp.exp(log_w - m_new[..., None])
        C_new = decay[..., None, None] * C + jnp.einsum('bhs,bhsv,bhsk->bhvk', w, vt, kt)
        n_new = decay[..., None] * n + jnp.einsum('bhs,bhsk->bhk', w, kt)
        return (C_new, n_new, m_new), h

    init = (jnp.zeros((B, H, d, d), jnp.float32),
            jnp.zeros((B, H, d), jnp.float32),
            jnp.full((B, H), M_INIT, jnp.float32))
    _, hs = lax.scan(step, init, (qc, kc, vc, ic, fc))
    return hs.transpose(1, 2, 0, 3, 4).reshape(B, H, S, d)

def setup_inputs(seed: int = 0) -> dict:
    key = jax.random.key(seed)
    ks = jax.random.split(key, 24)
    f32 = jnp.float32
    nrm = lambda k, shape, fan_in, s=1.0: jax.random.normal(k, shape, f32) * (s * fan_in ** -0.5)
    gain = lambda k, shape: 1.0 + 0.05 * jax.random.normal(k, shape, f32)
    gate_base = jnp.concatenate([jnp.zeros((N_MLSTM_HEADS,), f32), jnp.linspace(3.0, 6.0, N_MLSTM_HEADS, dtype=f32),
                                 jnp.zeros((N_MLSTM_HEADS,), f32), jnp.linspace(3.0, 6.0, N_MLSTM_HEADS, dtype=f32)])
    return {
        "x": jax.random.normal(ks[0], (BATCH, SEQ, D_MODEL), f32),
        "c": jax.random.normal(ks[1], (BATCH, D_MODEL), f32),
        "positions": jnp.broadcast_to(jnp.arange(SEQ, dtype=jnp.int32), (BATCH, SEQ)),
        "w_ada": nrm(ks[2], (DEPTH, D_MODEL, 6 * D_MODEL), D_MODEL, 0.5),
        "b_ada": 0.02 * jax.random.normal(ks[3], (DEPTH, 6 * D_MODEL), f32),
        "norm_mix_g": gain(ks[4], (DEPTH, D_MODEL)),
        "w_in": nrm(ks[5], (DEPTH, D_MODEL, D_IN), D_MODEL),
        "b_gates": gate_base + 0.1 * jax.random.normal(ks[6], (DEPTH, N_GATE_COLS), f32),
        "conv_w": nrm(ks[7], (DEPTH, CONV_WIDTH, 2 * MLSTM_WIDTH), CONV_WIDTH),
        "conv_b": 0.02 * jax.random.normal(ks[8], (DEPTH, 2 * MLSTM_WIDTH), f32),
        "q_lora_g": gain(ks[9], (DEPTH, Q_LORA)),
        "w_uq": nrm(ks[10], (DEPTH, Q_LORA, N_MLA_HEADS * MLA_QK_DIM), Q_LORA),
        "kv_lora_g": gain(ks[11], (DEPTH, KV_LORA)),
        "w_ukv": nrm(ks[12], (DEPTH, KV_LORA, N_MLA_HEADS * (MLA_NOPE_DIM + MLA_V_DIM)), KV_LORA),
        "q_norm_g": gain(ks[13], (DEPTH, MLA_QK_DIM)),
        "k_norm_g": gain(ks[14], (DEPTH, MLA_QK_DIM)),
        "mlstm_norm_g": gain(ks[15], (DEPTH, N_MLSTM_HEADS, MLSTM_HEAD_DIM)),
        "w_out": nrm(ks[16], (DEPTH, D_MIX, D_MODEL), D_MIX),
        "norm_mlp_g": gain(ks[17], (DEPTH, D_MODEL)),
        "w_ff1": nrm(ks[18], (DEPTH, D_MODEL, D_FF), D_MODEL),
        "w_ff2": nrm(ks[19], (DEPTH, D_FF, D_MODEL), D_FF),
    }

def reference(x, c, positions, w_ada, b_ada, norm_mix_g, w_in, b_gates, conv_w, conv_b,
              q_lora_g, w_uq, kv_lora_g, w_ukv, q_norm_g, k_norm_g, mlstm_norm_g,
              w_out, norm_mlp_g, w_ff1, w_ff2):
    B, S, D = x.shape
    H, HM, DM = N_MLA_HEADS, N_MLSTM_HEADS, MLSTM_HEAD_DIM
    for l in range(DEPTH):
        mod = jax.nn.silu(c) @ w_ada[l] + b_ada[l]
        shift1, scale1, gate1, shift2, scale2, gate2 = jnp.split(mod[:, None, :], 6, axis=-1)

        h = modulate(rmsnorm(x, norm_mix_g[l]), shift1, scale1)
        proj = h @ w_in[l]
        c_q, c_kv, k_pe, q_m, k_m, v_m, o_m, g_m = jnp.split(proj, IN_SPLIT_POINTS, axis=-1)

        q = (rmsnorm(c_q, q_lora_g[l]) @ w_uq[l]).reshape(B, S, H, MLA_QK_DIM)
        kv = (rmsnorm(c_kv, kv_lora_g[l]) @ w_ukv[l]).reshape(B, S, H, MLA_NOPE_DIM + MLA_V_DIM)
        k_nope, v = kv[..., :MLA_NOPE_DIM], kv[..., MLA_NOPE_DIM:]
        k_full = jnp.concatenate([k_nope, jnp.broadcast_to(k_pe[:, :, None, :], (B, S, H, ROPE_DIM))], axis=-1)
        q = rmsnorm(q, q_norm_g[l])
        k_full = rmsnorm(k_full, k_norm_g[l])
        q = jnp.concatenate([q[..., :MLA_NOPE_DIM], rope(q[..., MLA_NOPE_DIM:], positions)], axis=-1)
        k_full = jnp.concatenate([k_full[..., :MLA_NOPE_DIM], rope(k_full[..., MLA_NOPE_DIM:], positions)], axis=-1)
        attn_out = dense_attention_blocks(q, k_full, v)

        qk = jnp.concatenate([q_m, k_m], axis=-1)
        qk = lax.conv_general_dilated(qk, conv_w[l][:, None, :].astype(qk.dtype), window_strides=(1,),
                                      padding='SAME', dimension_numbers=('NWC', 'WIO', 'NWC'),
                                      feature_group_count=2 * MLSTM_WIDTH)
        qk = jax.nn.silu(qk + conv_b[l])
        to_heads = lambda t: t.reshape(B, S, HM, DM).transpose(0, 2, 1, 3).astype(jnp.float32)
        qh = to_heads(qk[..., :MLSTM_WIDTH])
        kh = to_heads(qk[..., MLSTM_WIDTH:]) * (DM ** -0.5)
        vh = to_heads(v_m)
        gates = (g_m.astype(jnp.float32) + b_gates[l].astype(jnp.float32)).reshape(B, S, 4, HM)
        gates = gates.transpose(2, 0, 3, 1)
        i_fwd, f_fwd, i_bwd, f_bwd = gates[0], gates[1], gates[2], gates[3]
        h_fwd = mlstm_chunkwise(qh, kh, vh, i_fwd, jax.nn.log_sigmoid(f_fwd))
        flip = lambda t: jnp.flip(t, axis=2)
        h_bwd = flip(mlstm_chunkwise(flip(qh), flip(kh), flip(vh), flip(i_bwd), flip(jax.nn.log_sigmoid(f_bwd))))
        hm = (h_fwd + h_bwd).transpose(0, 2, 1, 3)
        hm = rmsnorm(hm, mlstm_norm_g[l]).astype(x.dtype)
        mlstm_out = (jax.nn.sigmoid(o_m).reshape(B, S, HM, DM) * hm).reshape(B, S, MLSTM_WIDTH)

        mixed = jnp.concatenate([attn_out.astype(x.dtype), mlstm_out], axis=-1) @ w_out[l]
        x = x + gate1 * mixed

        h2 = modulate(rmsnorm(x, norm_mlp_g[l]), shift2, scale2)
        y = jnp.square(jax.nn.relu(h2 @ w_ff1[l])) @ w_ff2[l]
        x = x + gate2 * y
    return x


_drawn_inputs = setup_inputs


def setup_inputs(seed=0):
    import zlib

    import numpy as np

    out = dict(_drawn_inputs(seed))
    spreads = {}
    factors = {'norm_mix_g': 8.0,
     'conv_b': 64.0,
     'q_lora_g': 8.0,
     'w_uq': 3.527,
     'kv_lora_g': 8.0,
     'q_norm_g': 8.0,
     'k_norm_g': 8.0,
     'mlstm_norm_g': 8.0,
     'norm_mlp_g': 5.34}
    for name, (base, spread) in spreads.items():
        noise = np.random.default_rng([zlib.crc32(name.encode()), seed]).standard_normal(out[name].shape)
        drawn = base * np.exp(spread * noise) if base else spread * noise
        out[name] = __import__('jax').numpy.asarray(drawn.astype(out[name].dtype))
    for name, factor in factors.items():
        out[name] = (out[name] * factor).astype(out[name].dtype)
    return out
```

```python
from contextlib import ExitStack

import numpy as np

import concourse.bass as bass
from concourse import mybir

F = mybir.dt.float32
R = mybir.dt.float32r
I32 = mybir.dt.int32
ALU = mybir.AluOpType
ACT = mybir.ActivationFunctionType
AX = mybir.AxisListType

P = 128
D = 2048
S = 512
KT = D // P
TT = S // P
NH, NOPE, ROPE, VD = 8, 128, 64, 128
QK = NOPE + ROPE
QL, KVL = 512, 256
HM, DM = 4, 256
MW = HM * DM
DFF = 4 * D
W1ROWS = 512 + 256 + 64
DIN = QL + KVL + ROPE + 4 * MW + 4 * HM
EPS = 1e-6
NEG = -3.0e38
KB = 2
RING = 4
GB = KT // KB

G_IN = 10
N_MLA = G_IN * GB
PAIRS = NH // 2
N_OUT = N_MLA + 4 * PAIRS
G_OUT = D // 512
N_FF = N_OUT + G_OUT * GB
CH = 1024
CHUNKS = DFF // CH
CT = CH // P
CB = CH // 512 * GB + G_OUT * (CT // KB)

V_C, V_GMIX, V_GMLP, V_CB, V_QG, V_KVG, V_MG = 0, 16, 32, 48, 64, 68, 70
V_ROWS = 78
V_ADA = V_ROWS
V_CW = V_ADA + 96
V_POS = V_CW + 80
V_ALL = V_POS + TT
M_SH1, M_SC1, M_G1, M_SH2, M_SC2, M_G2 = 0, 16, 32, 48, 64, 80


def rope_freqs():
    half = ROPE // 2
    return np.float32(10000.0) ** (-np.arange(half, dtype=np.float32) / np.float32(half))


def build(nc, x, c, positions, w_ada, b_ada, norm_mix_g, w_in, b_gates, conv_w, conv_b,
          q_lora_g, w_uq, kv_lora_g, w_ukv, q_norm_g, k_norm_g, mlstm_norm_g,
          w_out, norm_mlp_g, w_ff1, w_ff2, out):
    perm = ExitStack()

    def at(stack, name, shape, dt=F):
        return stack.enter_context(nc.sbuf_tensor(name, shape, dt))

    def sem(name):
        return perm.enter_context(nc.semaphore(name))

    xT_d = nc.dram_tensor("xT_d", (P, KT, S), F, kind="Internal").ap()
    qk_d = nc.dram_tensor("qk_d", (2, P, 2 * MW // P, S), F, kind="Internal").ap()
    v_d = nc.dram_tensor("v_d", (2, P, TT, MW), F, kind="Internal").ap()
    o_d = nc.dram_tensor("o_d", (P, MW // P, S), F, kind="Internal").ap()
    g_d = nc.dram_tensor("g_d", (HM, 2, S), F, kind="Internal").ap()

    wraw = at(perm, "wraw", [P, RING, KB, 512])
    whi = at(perm, "whi", [P, RING, KB, 512], R)
    wlo = at(perm, "wlo", [P, RING, KB, 512], R)
    ident = at(perm, "ident", [P, P])
    ones = at(perm, "ones", [P, P])
    mask = at(perm, "mask", [P, 2, P])
    VT = at(perm, "VT", [P, V_ALL])
    M = at(perm, "M", [P, 96])
    silc = at(perm, "silc", [P, KT])
    A1 = at(perm, "A1", [P, KT])
    freq = at(perm, "freq", [P, ROPE // 2])
    cosT = at(perm, "cosT", [P, TT, ROPE // 2])
    sinT = at(perm, "sinT", [P, TT, ROPE // 2])
    qg = at(perm, "qg", [P, QK])
    kg = at(perm, "kg", [P, QK])
    bgate = at(perm, "bgate", [HM, 4])
    wgate = at(perm, "wgate", [P, KT, 16])
    rp = at(perm, "rp", [P, TT, ROPE])
    ssq = at(perm, "ssq", [P, 16])
    rs = at(perm, "rs", [P, 16])
    pess = at(perm, "pess", [P, TT])
    nhalf = at(perm, "nhalf", [P, 1])
    epsc = at(perm, "epsc", [P, 1])

    with ExitStack() as st:
        xnat = at(st, "xnat", [P, 2, D])
        sqacc = at(st, "sqacc", [P, S])
        rstd = at(st, "rstd", [P, S])
        utmp = at(st, "utmp", [P, 2, S])
        rows0 = at(st, "rows0", [V_ROWS, P])
        rows1 = at(st, "rows1", [96, P])
        rows2 = at(st, "rows2", [80, P])
        posi = at(st, "posi", [TT, P], I32)
        posf = at(st, "posf", [TT, P])
    low = ExitStack()
    cqT = [at(low, f"cqT{i}", [P, QL // P, S], R) for i in range(2)]
    ckvT = [at(low, f"ckvT{i}", [P, KVL // P, S], R) for i in range(2)]
    ckv = at(low, "ckv", [P, TT, 336])
    with ExitStack() as st:
        hT = [at(st, f"hT{i}", [P, KT, S], R) for i in range(2)]
        araw = at(st, "araw", [P, 4, 2, 512])
        acc = at(st, "acc", [P, 4, 512])
        with ExitStack() as s2:
            xT = at(s2, "xT", [P, KT, S])
        with ExitStack() as s2:
            cq = at(s2, "cq", [P, TT, QL])
            yc = at(s2, "yc", [P, 2, S])
            sth = at(s2, "sth", [P, 2, S])
            stl = at(s2, "stl", [P, 2, S])
            ang = at(s2, "ang", [P, 6, TT, ROPE // 2])
    mixst = ExitStack()
    mixA = [at(mixst, f"mixA{i}", [P, NH, S], R) for i in range(2)]
    with ExitStack() as st:
        qn = at(st, "qn", [P, TT, 2, QK])
        qr = at(st, "qr", [P, TT, 2, ROPE])
        kn = at(st, "kn", [P, TT, 2, NOPE])
        kr = at(st, "kr", [P, TT, 2, ROPE])
        rt = at(st, "rt", [P, 4, TT, 2, ROPE // 2])
        vv = [at(st, f"vv{i}", [P, TT, 2, VD], R) for i in range(2)]
        qT = [at(st, f"qT{i}", [P, 3, S], R) for i in range(2)]
        kT = [at(st, f"kT{i}", [P, 3, S], R) for i in range(2)]
        pr = at(st, "pr", [P, 2, TT, S])
        pT = [at(st, f"pT{i}", [P, TT, S], R) for i in range(2)]
        nmax = at(st, "nmax", [P, 8])
        nms = at(st, "nms", [P, 8])
        den = at(st, "den", [P, 8])
        rden = at(st, "rden", [P, 8])
    mixM = [at(mixst, f"mixM{i}", [P, NH, S], R) for i in range(2)]
    with ExitStack() as st:
        mq = [at(st, f"mq{i}", [P, 2, S], R) for i in range(2)]
        mk = [at(st, f"mk{i}", [P, 2, S], R) for i in range(2)]
        wT = [at(st, f"wT{i}", [P, TT, S], R) for i in range(2)]
        mo = at(st, "mo", [P, 2, S])
        sf = at(st, "sf", [P, TT, S])
        sbw = at(st, "sbw", [P, TT, S])
        mden = at(st, "mden", [P, 2, TT])
        mden2 = at(st, "mden2", [P, 2, TT])
        mrd = at(st, "mrd", [P, 2, TT])
        gcol = at(st, "gcol", [P, 2, 2, TT, HM])
    with ExitStack() as st:
        x1T = at(st, "x1T", [P, KT, S])
        ah0 = at(st, "ah", [P, CT, S], R)
    mixst.close()
    with ExitStack() as st:
        h2T = [at(st, f"h2T{i}", [P, KT, S], R) for i in range(2)]
    with ExitStack() as st:
        yst = at(st, "yst", [P, 2, D])
    low.close()
    with ExitStack() as st:
        mv = [at(st, f"mv{i}", [P, TT, DM], R) for i in range(2)]
        gb = at(st, "gb", [P, 2, S])
        gbm = at(st, "gbm", [P, 2, S])
        et = at(st, "et", [P, 2, 640])
    gT = sf[0:HM, :, :]
    gw = sbw[0:HM, :, :]
    grw = mo[0:HM, :, :]
    msq = gbm
    with ExitStack() as st:
        al0 = at(st, "al", [P, CT, S], R)
        sqacc2 = at(st, "sqacc2", [P, S])
        rstd2 = at(st, "rstd2", [P, S])
        utmp2 = at(st, "utmp2", [P, 2, S])
        sq2 = at(st, "sq2", [P, 2, S])
    aT = [ah0, al0]
    ps = perm.enter_context(nc.psum_tensor("ps", [P, 8, 512], F))

    def mix(part, kt):
        return (mixA if kt < NH else mixM)[part][:, kt % NH, :]

    w_loaded = [sem(f"w_loaded{i}") for i in range(RING)]
    hi_ready, lo_ready, blk_done = sem("hi_ready"), sem("lo_ready"), sem("blk_done")
    vec_loaded, gate_loaded = sem("vec_loaded"), sem("gate_loaded")
    const_done, vec_T, vec_cols = sem("const_done"), sem("vec_T"), sem("vec_cols")
    pos_f = sem("pos_f")
    silc_done = sem("silc_done")
    x_loaded = [sem("x_loaded0"), sem("x_loaded1")]
    x_T, x_evac, sq_done, sq_added = sem("x_T"), sem("x_evac"), sem("sq_done"), sem("sq_added")
    ssq_bc, ms_done, rstd_done = sem("ssq_bc"), sem("ms_done"), sem("rstd_done")
    ada_loaded = [sem(f"ada_loaded{i}") for i in range(4)]
    ada_step, ada_summed, ada_read = sem("ada_step"), sem("ada_summed"), sem("ada_read")
    u_done, h_hi, h_lo = sem("u_done"), sem("h_hi"), sem("h_lo")
    xT_stored = sem("xT_stored")
    bank_free = [sem("bank_free0"), sem("bank_free1")]
    c_mid, c_silu, c_hi, c_lo = sem("c_mid"), sem("c_silu"), sem("c_hi"), sem("c_lo")
    staged = [sem("staged0"), sem("staged1")]
    low_sq, low_ms, low_rs, low_norm = sem("low_sq"), sem("low_ms"), sem("low_rs"), sem("low_norm")
    low_T, low_hi, low_lo = sem("low_T"), sem("low_hi"), sem("low_lo")
    ang_r, trig = sem("ang_r"), sem("trig")
    dve_step, act_step, pool_step = sem("dve_step"), sem("act_step"), sem("pool_step")
    tap_step, sq_zero, dve_r = sem("tap_step"), sem("sq_zero"), sem("dve_r")
    a_sq, a_ms, a_rs, a_vhi, a_norm = sem("a_sq"), sem("a_ms"), sem("a_rs"), sem("a_vhi"), sem("a_norm")
    a_T, a_Thi, a_Tlo = sem("a_T"), sem("a_Thi"), sem("a_Tlo")
    a_S, a_max, a_exp, a_prob = sem("a_S"), sem("a_max"), sem("a_exp"), sem("a_prob")
    a_PT, a_PThi, a_PTlo, a_PV = sem("a_PT"), sem("a_PThi"), sem("a_PTlo"), sem("a_PV")
    a_ohi, a_olo = sem("a_ohi"), sem("a_olo")
    g_T, g_bias, g_exp, g_ln, g_rows, g_em = (sem("g_T"), sem("g_bias"), sem("g_exp"), sem("g_ln"),
                                              sem("g_rows"), sem("g_em"))
    g_stored, g_colT, g_cols = sem("g_stored"), sem("g_colT"), sem("g_cols")
    m_qk_in, m_v_in, m_g_in = sem("m_qk_in"), sem("m_v_in"), sem("m_g_in")
    m_mask, m_exp, m_S, m_sc, m_rd, m_w = (sem("m_mask"), sem("m_exp"), sem("m_S"), sem("m_sc"),
                                           sem("m_rd"), sem("m_w"))
    m_QK, m_WT, m_WThi, m_WTlo, m_V = sem("m_QK"), sem("m_WT"), sem("m_WThi"), sem("m_WTlo"), sem("m_V")
    m_sq, m_ss, m_ms, m_rs, m_t2, m_ohi, m_olo = (sem("m_sq"), sem("m_ss"), sem("m_ms"), sem("m_rs"),
                                                  sem("m_t2"), sem("m_ohi"), sem("m_olo"))
    xT_back, o_free, x1_done, o_sq, o_sqadd = (sem("xT_back"), [sem("o_free0"), sem("o_free1")],
                                               sem("x1_done"), sem("o_sq"), sem("o_sqadd"))
    o_ss, o_ms, o_rs, u2_done, h2_hi, h2_lo = (sem("o_ss"), sem("o_ms"), sem("o_rs"), sem("u2_done"),
                                               sem("h2_hi"), sem("h2_lo"))
    f_free = [sem("f_free0"), sem("f_free1")]
    f_relu, f_sq, f_hi, f_lo = sem("f_relu"), sem("f_sq"), sem("f_hi"), sem("f_lo")
    y_T, y_act, y_dve = sem("y_T"), sem("y_act"), sem("y_dve")
    y_stored = [sem("y_stored0"), sem("y_stored1")]

    w_in3 = w_in.rearrange("(k p) n -> p k n", p=P)
    w_ada3 = w_ada.rearrange("(k p) n -> p k n", p=P)
    w_uq3 = w_uq.rearrange("(k p) n -> p k n", p=P)
    w_ukv3 = w_ukv.rearrange("(k p) n -> p k n", p=P)
    w_out3 = w_out.rearrange("(k p) n -> p k n", p=P)
    w_ff13 = w_ff1.rearrange("(k p) n -> p k n", p=P)
    w_ff23 = w_ff2.rearrange("(k p) n -> p k n", p=P)

    def one(tile, i):
        return tile[:, bass.ds(i, 1), :].rearrange("p a n -> p (a n)")

    def col(tile, i):
        return tile[:, bass.ds(i, 1)]

    block = perm.enter_context(nc.Block())

    def load_block(sp, n, slot, src, cols=512, kb=KB, first=False):
        if not first:
            sp.wait_ge(lo_ready, n - RING + 1)
        sp.dma_start(wraw[:, slot, 0:kb, 0:cols], src).then_inc(w_loaded[slot], 16)

    def split_hi(act, n, slot, use, cols=512, kb=KB, first=False):
        act.wait_ge(w_loaded[slot], 16 * use)
        if not first:
            act.wait_ge(blk_done, n - RING + 1)
        act.activation(whi[:, slot, 0:kb, 0:cols], wraw[:, slot, 0:kb, 0:cols],
                       ACT.Copy).then_inc(hi_ready, 1)

    def split_lo(pool, n, slot, cols=512, kb=KB):
        pool.wait_ge(hi_ready, n + 1)
        pool.tensor_tensor(wlo[:, slot, 0:kb, 0:cols], wraw[:, slot, 0:kb, 0:cols],
                           whi[:, slot, 0:kb, 0:cols].bitcast(F), ALU.subtract).then_inc(lo_ready, 1)

    def ada_unit_release(pair, u):
        return 32 * pair + 4 * (u // 2) + 3 + u % 2

    @block.sync
    def _(sp):
        vr = lambda ap: ap.rearrange("(a p) -> a p", p=P)
        loads = [
            (rows0[V_C:V_C + 16, :], vr(c)), (rows0[V_GMIX:V_GMIX + 16, :], vr(norm_mix_g)),
            (rows0[V_GMLP:V_GMLP + 16, :], vr(norm_mlp_g)), (rows0[V_CB:V_CB + 16, :], vr(conv_b)),
            (rows0[V_QG:V_QG + 4, :], vr(q_lora_g)), (rows0[V_KVG:V_KVG + 2, :], vr(kv_lora_g)),
            (rows0[V_MG:V_MG + 8, :], vr(mlstm_norm_g)), (rows1[:, :], vr(b_ada)),
            (rows2[:, :], vr(conv_w)), (posi[:, :], vr(positions)),
            (qg[:, :], q_norm_g.partition_broadcast(P)), (kg[:, :], k_norm_g.partition_broadcast(P)),
            (bgate[:, :], b_gates.rearrange("(k h) -> h k", h=HM)),
        ]
        for dst, src in loads:
            sp.dma_start(dst, src, allow_slow_non_contiguous=dst.tensor.name == "bgate").then_inc(vec_loaded, 16)
        sp.dma_start(wgate[:, :, :], w_in3[:, :, DIN - 16:DIN]).then_inc(gate_loaded, 16)

        def ada_load(pair, u, col0, col1, first=False):
            if not first:
                if u >= 4:
                    sp.wait_ge(ada_step, ada_unit_release(pair, u - 4))
                else:
                    sp.wait_ge(ada_step, ada_unit_release(pair - 1, u + 12))
            k0 = 2 * (u // 2)
            sp.dma_start(araw[:, u % 4, :, :],
                         w_ada3[:, k0:k0 + 2, bass.ds((col0, col1)[u % 2], 512)]
                         ).then_inc(ada_loaded[u % 4], 16)

        def in_load(n, first=False):
            g, b = n // GB, n % GB
            cols = 320 if g == 1 else 512
            src = w_in3[:, KB * b:KB * b + KB, 512 * g:512 * g + cols]
            load_block(sp, n, n % RING, src, cols, first=first)

        for q in range(4):
            for u in range(16):
                ada_load(q, u, 512 * q, D + 512 * q, first=(q == 0 and u < 4))
            if q == 0:
                for n in range(4):
                    in_load(n, first=True)
            else:
                in_load(2 * q + 2)
                in_load(2 * q + 3)
        for b in range(2, 8):
            in_load(8 + b)
            if b >= 4:
                for u in (2 * b - 8, 2 * b - 7):
                    ada_load(4, u, 2 * D, 2 * D + 512)

        def in_group(g, ada):
            for b in range(GB):
                load_block(sp, GB * g + b, b % RING,
                           w_in3[:, KB * b:KB * b + KB, bass.ds(W1ROWS + 512 * (g - 2), 512)])
                pr_, u0 = (g + 2, 2 * b + 8) if b < 4 else (g + 3, 2 * b - 8)
                if b < 4 or ada:
                    for u in (u0, u0 + 1):
                        col0 = 2 * D + 1024 * (pr_ - 4)
                        ada_load(pr_, u, col0, col0 + 512)
        with sp.Fori(2, 9) as g:
            in_group(g, True)
        in_group(9, False)

        with sp.Fori(0, PAIRS) as p:
            for i in range(2):
                load_block(sp, N_MLA + 4 * p + i, i,
                           w_uq3[:, 2 * i:2 * i + 2, bass.ds(2 * QK * p, 2 * QK)], 2 * QK)
            for i in range(2):
                load_block(sp, N_MLA + 4 * p + 2 + i, 2 + i,
                           w_ukv3[:, i:i + 1, bass.ds(512 * p, 512)], 512, 1)

        def out_load(g, b):
            load_block(sp, N_OUT + GB * g + b, b % RING,
                       w_out3[:, KB * b:KB * b + KB, bass.ds(512 * g, 512)])
        for b in range(3):
            out_load(0, b)

        for s in range(2):
            sp.wait_ge(staged[s], 32 * 12 + 16 * 4)
        sp.wait_ge(a_olo, NH)
        sp.wait_ge(g_rows, 1)
        sp.dma_start(g_d.rearrange("h d s -> h d s"), grw).then_inc(g_stored, 16)
        sp.wait_ge(g_stored, 16)

        def head_load(h, first=False):
            if not first:
                sp.wait_ge(m_QK, TT * h)
            for part in range(2):
                sp.dma_start(mq[part][:, :, :].bitcast(F), qk_d[part, :, bass.ds(2 * h, 2), :]
                             ).then_inc(m_qk_in, 16)
                sp.dma_start(mk[part][:, :, :].bitcast(F), qk_d[part, :, bass.ds(8 + 2 * h, 2), :]
                             ).then_inc(m_qk_in, 16)
            if not first:
                sp.wait_ge(m_S, 2 * TT * h)
            sp.dma_start(gb[:, :, :], g_d[bass.ds(h, 1)].rearrange("a d s -> (a d s)")
                         .partition_broadcast(P).rearrange("p (d s) -> p d s", d=2)).then_inc(m_g_in, 16)
            if not first:
                sp.wait_ge(m_olo, 2 * h)
            for part in range(2):
                sp.dma_start(mv[part][:, :, :].bitcast(F), v_d[part, :, :, bass.ds(DM * h, DM)]
                             ).then_inc(m_v_in, 16)
            sp.dma_start(mo[:, :, :], o_d[:, bass.ds(2 * h, 2), :]).then_inc(m_v_in, 16)
        head_load(0, True)
        with sp.Fori(1, HM) as h:
            head_load(h)

        sp.wait_ge(m_olo, 2 * HM)
        sp.wait_ge(xT_stored, 16)
        sp.dma_start(x1T[:, :, :], xT_d).then_inc(xT_back, 16)
        for b in range(3, GB):
            out_load(0, b)
        with sp.Fori(1, G_OUT) as g:
            for b in range(GB):
                out_load(g, b)

        with sp.Fori(0, CHUNKS) as ch:
            for q in range(2):
                for b in range(GB):
                    load_block(sp, N_FF + CB * ch + GB * q + b, b % RING,
                               w_ff13[:, KB * b:KB * b + KB, bass.ds(CH * ch + 512 * q, 512)])
            for q in range(4):
                for b in range(CT // KB):
                    load_block(sp, N_FF + CB * ch + 2 * GB + 4 * q + b, b % RING,
                               w_ff23[:, bass.ds(CT * ch + KB * b, KB), 512 * q:512 * q + 512])

        for t in range(TT):
            sp.wait_ge(y_act, 2 * (t + 1))
            sp.wait_ge(y_dve, 2 * (t + 1))
            sp.dma_start(out[t * P:(t + 1) * P, :], yst[:, t % 2, :]).then_inc(y_stored[t % 2], 16)
        for s in range(2):
            sp.wait_ge(y_stored[s], 16 * TT // 2)

    @block.gpsimd
    def _(pool):
        steps = [0]

        def link(ins):
            steps[0] += 1
            ins.then_inc(pool_step, 1)
        link(pool.memset(ident[:, :], 0.0))
        link(pool.memset(mask[:, :, :], 0.0))
        for i, f in enumerate(rope_freqs()):
            link(pool.memset(freq[:, i:i + 1], float(f)))
        link(pool.memset(ones[:, :], 1.0))
        link(pool.memset(nhalf[:, :], -0.5))
        link(pool.memset(epsc[:, :], EPS))
        pool.wait_ge(pool_step, steps[0])
        pool.affine_select(out=ident[:, :], in_=ident[:, :], compare_op=ALU.not_equal, fill=1.0, base=0,
                           pattern=[[-1, P]], channel_multiplier=1).then_inc(const_done, 1)
        pool.affine_select(out=mask[:, 0, :], in_=mask[:, 0, :], compare_op=ALU.is_ge, fill=NEG, base=0,
                           pattern=[[-1, P]], channel_multiplier=1).then_inc(const_done, 1)
        pool.affine_select(out=mask[:, 1, :], in_=mask[:, 1, :], compare_op=ALU.is_ge, fill=NEG, base=0,
                           pattern=[[1, P]], channel_multiplier=-1).then_inc(const_done, 1)

        for k in range(4):
            pool.wait_ge(sq_done, k + 1)
            for j in range(4):
                sq = xnat[:, k % 2, j * S:(j + 1) * S]
                if k == 0 and j == 0:
                    pool.tensor_copy(sqacc[:, :], sq).then_inc(sq_added, 1)
                else:
                    pool.wait_ge(sq_added, 4 * k + j)
                    pool.tensor_tensor(sqacc[:, :], sqacc[:, :], sq, ALU.add).then_inc(sq_added, 1)
        pool.wait_ge(ms_done, 1)
        pool.tensor_tensor(rstd[:, :], utmp[:, 0, :], nhalf[:, 0:1].to_broadcast([P, S]),
                           ALU.pow).then_inc(rstd_done, 1)

        for n in range(3 * GB):
            split_lo(pool, n, n % RING, 336 if n // GB == 1 else 512)
            if n == 3 * GB - 1:
                pool.wait_ge(low_ms, 1)
                pool.tensor_tensor(rs[:, 0:8], ssq[:, 0:8], nhalf[:, 0:1].to_broadcast([P, 8]),
                                   ALU.pow).then_inc(low_rs, 1)
        with pool.Fori(3 * GB // 4, N_MLA // 4) as i:
            for s in range(4):
                split_lo(pool, 4 * i + s, s)
        with pool.Fori(0, PAIRS) as p:
            for i in range(2):
                split_lo(pool, N_MLA + 4 * p + i, i, 2 * QK)
            for i in range(2):
                split_lo(pool, N_MLA + 4 * p + 2 + i, 2 + i, 512, 1)
            pool.wait_ge(a_ms, p + 1)
            pool.tensor_tensor(rs[:, :], ssq[:, :], nhalf[:, 0:1].to_broadcast([P, 16]),
                               ALU.pow).then_inc(a_rs, 1)
        for s in range(3):
            split_lo(pool, N_OUT + s, s)
        with pool.Fori(0, HM) as h:
            pool.wait_ge(m_g_in, 16 * (h + 1))
            pool.wait_ge(m_olo, 2 * h)
            for d in range(2):
                pool.tensor_tensor(gbm[:, d, :].rearrange("p (a n) -> p a n", a=TT),
                                   gb[:, d, :].rearrange("p (a n) -> p a n", a=TT),
                                   mask[:, d, None, :].to_broadcast([P, TT, P]), ALU.add).then_inc(m_mask, 1)
            pool.wait_ge(m_ms, h + 1)
            pool.tensor_tensor(et[:, 0, 0:S], et[:, 0, 0:S], nhalf[:, 0:1].to_broadcast([P, S]),
                               ALU.pow).then_inc(m_rs, 1)
        split_lo(pool, N_OUT + 3, 3)
        with pool.Fori(1, GB * G_OUT // 4) as i:
            for s in range(4):
                split_lo(pool, N_OUT + 4 * i + s, s)
        for s in range(3):
            split_lo(pool, N_FF + s, s)
        pool.wait_ge(o_ms, 1)
        pool.tensor_tensor(rstd2[:, :], utmp2[:, 0, :], nhalf[:, 0:1].to_broadcast([P, S]),
                           ALU.pow).then_inc(o_rs, 1)
        split_lo(pool, N_FF + 3, 3)
        with pool.Fori(1, CB * CHUNKS // 4) as i:
            for s in range(4):
                split_lo(pool, N_FF + 4 * i + s, s)

    @block.tensor
    def _(pe):
        def passes(dst, lhs, rhs, start, stop):
            pe.matmul(dst, lhs[0], rhs[0], start=start, stop=False)
            pe.matmul(dst, lhs[0], rhs[1], start=False, stop=False)
            return pe.matmul(dst, lhs[1], rhs[0], start=False, stop=stop)

        def wtile(slot, k, lo, hi):
            return [t[:, slot, k, lo:hi] for t in (whi, wlo)]

        def group_block(n, b, half, act_of, blocks, by_tokens, cols=512, kready=None):
            slot = b % RING
            pe.wait_ge(lo_ready, n + 1)
            for k in range(KB):
                kt = KB * b + k
                if kready is not None:
                    kready(kt)
                for m in range(4):
                    first, last = kt == 0, kt == KB * blocks - 1
                    if by_tokens:
                        ins = passes(ps[:, 4 * half + m, 0:cols],
                                     [act_of(i, kt)[:, m * P:(m + 1) * P] for i in range(2)],
                                     wtile(slot, k, 0, cols), first, last)
                    else:
                        ins = passes(ps[:, 4 * half + m, :], wtile(slot, k, m * P, (m + 1) * P),
                                     [act_of(i, kt) for i in range(2)], first, last)
            ins.then_inc(blk_done, 1)

        def ada_sum(pair, parity, bank):
            pe.wait_ge(ada_step, 32 * (pair + 1))
            for w in range(2):
                for j in range(4):
                    ins = pe.matmul(ps[:, bank, 4 * w + j:4 * w + j + 1],
                                    acc[:, 2 * parity + w, j * P:(j + 1) * P], ones[:, 0:1],
                                    start=True, stop=True)
            ins.then_inc(ada_summed, 1)

        pe.wait_ge(const_done, 3)
        pe.wait_ge(vec_loaded, 16 * 13)
        pe.wait_ge(pos_f, 1)
        pe.transpose(ps[:, 7, 0:V_ROWS], rows0[:, :], ident[0:V_ROWS, 0:V_ROWS])
        pe.transpose(ps[:, 7, V_ADA:V_ADA + 96], rows1[:, :], ident[0:96, 0:96])
        pe.transpose(ps[:, 7, V_CW:V_CW + 80], rows2[:, :], ident[0:80, 0:80])
        pe.transpose(ps[:, 7, V_POS:V_POS + TT], posf[:, :], ident[0:TT, 0:TT]).then_inc(vec_T, 1)
        for t in range(TT):
            pe.wait_ge(x_loaded[t % 2], 16 * (t // 2 + 1))
            if t >= 2:
                pe.wait_ge(x_evac, 4 * (t - 1))
            if t == 1:
                pe.wait_ge(vec_cols, 1)
            for k in range(4):
                for j in range(4):
                    ft = 4 * k + j
                    ins = pe.transpose(ps[:, 4 * (t % 2) + k, j * P:(j + 1) * P],
                                       xnat[:, t % 2, ft * P:(ft + 1) * P], ident[:, :])
                ins.then_inc(x_T, 1)
        pe.wait_ge(sq_added, KT)
        pe.wait_ge(x_evac, 4 * TT)
        pe.matmul(ps[:, 4, :], ones[:, :], sqacc[:, :], start=True, stop=True).then_inc(ssq_bc, 1)

        hin = lambda i, kt: hT[i][:, kt, :]
        for q in range(4):
            if q >= 1:
                pe.wait_ge(ada_read, 2 * q)
            ada_sum(q, q % 2, 5)
            for b in (2 * q, 2 * q + 1):
                group_block(b, b, 0, hin, GB, True, kready=lambda kt: pe.wait_ge(h_lo, kt + 1))
        pe.wait_ge(ada_read, 8)
        for b in range(GB):
            group_block(GB + b, b, 1, hin, GB, True, cols=336)

        def in_pair(gp, by_tokens):
            for h in range(2):
                pe.wait_ge(bank_free[h], 4 * gp)
                pe.wait_ge(ada_read, 2 * (2 * gp + h + 2))
                for b in range(GB):
                    if b == 5:
                        pe.wait_ge(bank_free[1 - h], 4 * gp + 4 * h)
                        ada_sum(2 * gp + h + 2, h, 4 * (1 - h) + 3)
                    group_block(GB * (2 * gp + h) + b, b, h, hin, GB, by_tokens)
        with pe.Fori(1, 3) as gp:
            in_pair(gp, False)
        in_pair(3, True)
        in_pair(4, False)

        pe.wait_ge(bank_free[0], 20)
        pe.wait_ge(bank_free[1], 20)
        pe.wait_ge(ada_read, 24)
        pe.wait_ge(low_norm, 8)
        for ft in range(4):
            for t in range(TT):
                ins = pe.transpose(ps[:, ft, t * P:(t + 1) * P], cq[:, t, ft * P:(ft + 1) * P], ident[:, :])
            ins.then_inc(low_T, 1)
        for ft in range(2):
            for t in range(TT):
                ins = pe.transpose(ps[:, 4 + ft, t * P:(t + 1) * P], ckv[:, t, ft * P:(ft + 1) * P],
                                   ident[:, :])
            ins.then_inc(low_T, 1)
        pe.wait_ge(low_lo, 6)

        with pe.Fori(0, PAIRS) as p:
            n0 = N_MLA + 4 * p
            pe.wait_ge(a_olo, 2 * p)
            for i in range(2):
                pe.wait_ge(lo_ready, n0 + i + 1)
                for k in range(2):
                    kt = 2 * i + k
                    for t in range(TT):
                        ins = passes(ps[:, t, 0:2 * QK], [cqT[j][:, kt, t * P:(t + 1) * P] for j in range(2)],
                                     wtile(i, k, 0, 2 * QK), kt == 0, kt == 3)
                ins.then_inc(blk_done, 1)
            for i in range(2):
                pe.wait_ge(lo_ready, n0 + i + 3)
                for t in range(TT):
                    ins = passes(ps[:, 4 + t, :], [ckvT[j][:, i, t * P:(t + 1) * P] for j in range(2)],
                                 wtile(2 + i, 0, 0, 512), i == 0, i == 1)
                ins.then_inc(blk_done, 1)
            for which, (nat, rot) in enumerate(((qn, qr), (kn, kr))):
                pe.wait_ge(a_norm, 2 * p + which + 1)
                for h in range(2):
                    for t in range(TT):
                        pe.transpose(ps[:, 4 * which + h, t * P:(t + 1) * P], nat[:, t, h, 0:NOPE], ident[:, :])
                for t in range(TT):
                    ins = pe.transpose(ps[:, 4 * which + 2, t * P:(t + 1) * P],
                                       rot[:, t, :, :].rearrange("p h d -> p (h d)"), ident[:, :])
                ins.then_inc(a_T, 1)
            pe.wait_ge(a_Tlo, 2 * (p + 1))
            for h in range(2):
                for t in range(TT):
                    q = slice(t * P, (t + 1) * P)
                    r = slice(ROPE * h, ROPE * h + ROPE)
                    passes(ps[:, 4 * h + t, :], [qT[i][:, h, q] for i in range(2)],
                           [kT[i][:, h, :] for i in range(2)], True, False)
                    passes(ps[:, 4 * h + t, :], [qT[i][r, 2, q] for i in range(2)],
                           [kT[i][r, 2, :] for i in range(2)], False, True).then_inc(a_S, 1)
            for h in range(2):
                for t in range(TT):
                    pe.wait_ge(a_prob, 8 * p + 4 * h + t + 1)
                    for j in range(TT):
                        ins = pe.transpose(ps[:, 4 * h + t, j * P:(j + 1) * P],
                                           pr[:, h, t, j * P:(j + 1) * P], ident[:, :])
                    ins.then_inc(a_PT, 1)
                pe.wait_ge(a_PTlo, 8 * p + 4 * h + 4)
                for j in range(TT):
                    ins = passes(ps[:, 4 * h, :], [vv[i][:, j, h, :] for i in range(2)],
                                 [pT[i][:, j, :] for i in range(2)], j == 0, j == TT - 1)
                ins.then_inc(a_PV, 1)

        pe.wait_ge(a_olo, NH)
        for k in range(4):
            for t in range(TT):
                ins = pe.transpose(ps[0:HM, k, t * P:(t + 1) * P], ckv[:, t, 320 + 4 * k:324 + 4 * k],
                                   ident[:, :])
        ins.then_inc(g_T, 1)
        pe.wait_ge(g_rows, 1)
        pe.wait_ge(g_em, 1)
        for w in range(2):
            for d in range(2):
                for t in range(TT):
                    i = (w * 2 + d) * TT + t
                    ins = pe.transpose(ps[:, 7, HM * i:HM * i + HM],
                                       gT[:, 2 * w + d, t * P:(t + 1) * P], ident[0:HM, 0:HM])
        ins.then_inc(g_colT, 1)

        with pe.Fori(0, HM) as h:
            pe.wait_ge(m_qk_in, 64 * (h + 1))
            pe.wait_ge(m_S, 2 * TT * h)
            for t in range(TT):
                for k in range(2):
                    ins = passes(ps[:, t, :], [mq[i][:, k, t * P:(t + 1) * P] for i in range(2)],
                                 [mk[i][:, k, :] for i in range(2)], k == 0, k == 1)
                ins.then_inc(m_QK, 1)
            pe.wait_ge(m_olo, 2 * h)
            pe.wait_ge(g_cols, 1)
            for t in range(TT):
                pe.wait_ge(m_w, TT * h + t + 1)
                for j in range(TT):
                    ins = pe.transpose(ps[:, 4 + t, j * P:(j + 1) * P], sf[:, t, j * P:(j + 1) * P],
                                       ident[:, :])
                ins.then_inc(m_WT, 1)
            pe.wait_ge(m_v_in, 48 * (h + 1))
            pe.wait_ge(m_WTlo, TT * (h + 1))
            for v in range(2):
                for j in range(TT):
                    ins = passes(ps[:, 4 + v, :], [mv[i][:, j, v * P:(v + 1) * P] for i in range(2)],
                                 [wT[i][:, j, :] for i in range(2)], j == 0, j == TT - 1)
                ins.then_inc(m_V, 1)
            for v in range(2):
                pe.wait_ge(m_sq, 2 * h + v + 1)
                ins = pe.matmul(ps[:, 6, :], ones[:, :], msq[:, v, :], start=(v == 0), stop=(v == 1))
            ins.then_inc(m_ss, 1)

        pe.wait_ge(m_olo, 2 * HM)
        with pe.Fori(0, G_OUT // 2) as gp:
            for h in range(2):
                pe.wait_ge(o_free[h], 4 * gp)
                for b in range(GB):
                    group_block(N_OUT + GB * (2 * gp + h) + b, b, h, mix, GB, False)
        pe.wait_ge(o_sqadd, KT)
        pe.wait_ge(o_free[0], 8)
        pe.matmul(ps[:, 0, :], ones[:, :], sqacc2[:, :], start=True, stop=True).then_inc(o_ss, 1)
        pe.wait_ge(o_free[1], 8)
        pe.wait_ge(o_ms, 1)

        with pe.Fori(0, CHUNKS) as ch:
            for q in range(2):
                pe.wait_ge(f_free[q], 12 * ch)
                for b in range(GB):
                    group_block(N_FF + CB * ch + GB * q + b, b, q, lambda i, kt: h2T[i][:, kt, :], GB, False,
                                kready=(lambda kt: pe.wait_ge(h2_lo, kt + 1)) if q == 0 else None)
            for q in range(4):
                pe.wait_ge(f_free[q % 2], 12 * ch + 4 * (q // 2 + 1))
                for b in range(CT // KB):
                    group_block(N_FF + CB * ch + 2 * GB + 4 * q + b, b, q % 2,
                                lambda i, kt: aT[i][:, kt, :], CT // KB, False,
                                kready=(lambda kt: pe.wait_ge(f_lo, CT * ch + kt + 1)) if q == 0 else None)

        pe.wait_ge(f_free[0], 12 * CHUNKS)
        pe.wait_ge(f_free[1], 12 * CHUNKS)
        for t in range(TT):
            if t >= 2:
                pe.wait_ge(y_act, 2 * (t - 1))
                pe.wait_ge(y_dve, 2 * (t - 1))
            for k in range(4):
                for j in range(4):
                    ins = pe.transpose(ps[:, 4 * (t % 2) + k, j * P:(j + 1) * P],
                                       x1T[:, 4 * k + j, t * P:(t + 1) * P], ident[:, :])
                ins.then_inc(y_T, 1)

    @block.scalar
    def _(act):
        for t in range(2):
            act.dma_start(xnat[:, t, :], x[t * P:(t + 1) * P, :]).then_inc(x_loaded[t], 16)
        act.wait_ge(vec_cols, 1)
        act.activation(silc[:, :], VT[:, V_C:V_C + KT], ACT.Silu).then_inc(silc_done, 1)
        for t in range(TT):
            for k in range(4):
                act.wait_ge(x_T, 4 * t + k + 1)
                if t < 2 and k == 3:
                    act.dma_start(xnat[:, t, :], x[(t + 2) * P:(t + 3) * P, :]).then_inc(x_loaded[t], 16)
                act.activation(xT[:, 4 * k:4 * k + 4, t * P:(t + 1) * P],
                               ps[:, 4 * (t % 2) + k, :].rearrange("p (j n) -> p j n", j=4),
                               ACT.Copy).then_inc(x_evac, 1)
        act.wait_ge(x_evac, 4 * TT)
        for k in range(4):
            if k >= 2:
                act.wait_ge(sq_added, 4 * (k - 1))
            act.activation(xnat[:, k % 2, :], xT[:, 4 * k:4 * k + 4, :].rearrange("p a n -> p (a n)"),
                           ACT.Square).then_inc(sq_done, 1)

        def in_split(n):
            g = n // GB
            slot, use = n % RING, n // RING + 1
            if g != 1:
                split_hi(act, n, slot, use, first=n < RING)
                return
            act.wait_ge(w_loaded[slot], 16 * use)
            act.wait_ge(blk_done, n - RING + 1)
            act.wait_ge(gate_loaded, 16)
            b = n % GB
            act.activation(wraw[:, slot, :, 320:336], wgate[:, KB * b:KB * b + KB, :],
                           ACT.Copy).then_inc(act_step, 1)
            gsteps[0] += 1
            act.wait_ge(act_step, gsteps[0])
            act.activation(whi[:, slot, :, 0:336], wraw[:, slot, :, 0:336], ACT.Copy).then_inc(hi_ready, 1)
        gsteps = [0]

        for n in range(3):
            in_split(n)
        for q in range(4):
            for k in range(4 * q, 4 * q + 4):
                act.wait_ge(u_done, k + 1)
                act.activation(hT[0][:, k, :], utmp[:, k % 2, :], ACT.Identity,
                               bias=M[:, M_SH1 + k:M_SH1 + k + 1]).then_inc(h_hi, 1)
            in_split(2 * q + 3)
            in_split(2 * q + 4)
        act.wait_ge(h_lo, KT)
        act.dma_start(xT_d, xT[:, :, :]).then_inc(xT_stored, 16)

        for b in range(GB):
            in_split(GB + b + 3)
            if b < TT:
                act.wait_ge(blk_done, GB)
                act.wait_ge(xT_stored, 16)
                act.activation(cq[:, b, :], ps[:, b, :], ACT.Copy).then_inc(bank_free[0], 1)
        act.wait_ge(ang_r, 1)
        act.activation(sinT[:, :, :], ang[:, 4, :, :], ACT.Sin).then_inc(trig, 1)
        act.activation(cosT[:, :, :], ang[:, 5, :, :], ACT.Sin).then_inc(trig, 1)
        for b in range(GB):
            in_split(2 * GB + b + 3)
            if b < TT:
                act.wait_ge(blk_done, 2 * GB)
                act.activation(ckv[:, b, :], ps[:, 4 + b, 0:336], ACT.Copy).then_inc(bank_free[1], 1)
            if b == 4:
                act.wait_ge(bank_free[0], 4)
                act.wait_ge(bank_free[1], 4)
                junk = sth[:, :, :].rearrange("p a n -> p (a n)")
                for t in range(TT):
                    j = 336 * (t % 2)
                    if t >= 2:
                        act.wait_ge(low_sq, 3 * (t - 1))
                    act.activation(stl[:, t % 2, :], cq[:, t, :], ACT.Square,
                                   accum_out=ssq[:, t:t + 1]).then_inc(low_sq, 1)
                    act.activation(junk[:, j:j + 256], ckv[:, t, 0:256], ACT.Square,
                                   accum_out=ssq[:, 4 + t:5 + t]).then_inc(low_sq, 1)
                    act.activation(junk[:, j + 256:j + 320], ckv[:, t, 256:320], ACT.Square,
                                   accum_out=pess[:, t:t + 1]).then_inc(low_sq, 1)

        def store(T, i, qk):
            act.wait_ge(c_lo, T + 1)
            for part, buf in enumerate((sth, stl)):
                if qk:
                    d = qk_d[part, :, bass.ds(T, 1), :].rearrange("p a n -> p (a n)")
                else:
                    d = v_d[part, :, i, 512 * ((T - 16) // 4):512 * ((T - 16) // 4) + 512]
                act.dma_start(d, buf[:, i % 2, :]).then_inc(staged[i % 2], 16)

        def conv_group(g, half, gp):
            T0 = 4 * (g - 3)
            for b in range(GB):
                n = GB * g + b + 3
                split_hi(act, n, (b + 3) % RING, 2 * g + (b + 3) // RING + 1)
                if b < 4:
                    act.wait_ge(blk_done, GB * g)
                    if b >= 2:
                        act.wait_ge(c_lo, T0 + b - 1)
                    else:
                        act.wait_ge(c_lo, T0)
                    act.activation(yc[:, b % 2, :], ps[:, 4 * half + b, :], ACT.Identity,
                                   scale=col(VT, V_CW + 32 + T0 + b), bias=col(VT, V_CB + T0 + b)
                                   ).then_inc(c_mid, 1)
                if 1 <= b <= 4:
                    i = b - 1
                    act.wait_ge(bank_free[half], 4 * gp + i + 1)
                    act.activation(yc[:, i % 2, :], yc[:, i % 2, :], ACT.Silu).then_inc(c_silu, 1)
                    act.wait_ge(c_silu, T0 + i + 1)
                    act.wait_ge(staged[i % 2], 16 * (T0 + 2 * (i // 2)))
                    act.activation(sth[:, i % 2, :].bitcast(R), yc[:, i % 2, :], ACT.Copy).then_inc(c_hi, 1)
                if 2 <= b <= 5:
                    store(T0 + b - 2, (b - 2) % 4, True)

        act.wait_ge(low_sq, 12)
        with act.Fori(1, 3) as gp:
            conv_group(2 * gp + 1, 0, gp)
            conv_group(2 * gp + 2, 1, gp)

        def v_group(g, half):
            T0 = 4 * (g - 3)
            for b in range(GB):
                n = GB * g + b + 3
                split_hi(act, n, (b + 3) % RING, 2 * g + (b + 3) // RING + 1)
                if b < 4:
                    act.wait_ge(blk_done, GB * g)
                    act.wait_ge(staged[b % 2], 16 * (T0 + 2 * (b // 2)))
                    act.activation(sth[:, b % 2, :].bitcast(R), ps[:, 4 * half + b, :], ACT.Copy
                                   ).then_inc(c_hi, 1)
                if 1 <= b <= 4:
                    store(T0 + b - 1, b - 1, False)

        def o_group(g, half):
            for b in range(GB):
                n = GB * g + b + 3
                if n < N_MLA:
                    split_hi(act, n, (b + 3) % RING, 2 * g + (b + 3) // RING + 1)
                if b < 4:
                    i = 4 * (g - 9) + b
                    act.wait_ge(blk_done, GB * g)
                    act.wait_ge(staged[b % 2], 32 * 12 + 16 * (i // 2))
                    act.activation(sth[:, b % 2, :], ps[:, 4 * half + b, :], ACT.Sigmoid
                                   ).then_inc(bank_free[half], 1)
                    act.wait_ge(bank_free[half], 16 + b + 1)
                    act.dma_start(o_d[:, i, :], sth[:, b % 2, :]).then_inc(staged[b % 2], 16)
        v_group(7, 0)
        v_group(8, 1)
        o_group(9, 0)
        def mla_split(p, i):
            n = N_MLA + 4 * p + i
            split_hi(act, n, i, N_MLA // RING + p + 1, 2 * QK if i < 2 else 512, 2 if i < 2 else 1)
        o_group(10, 1)

        for s in range(2):
            act.wait_ge(staged[s], 32 * 12 + 16 * 4)
        for ft in range(6):
            act.wait_ge(low_T, ft + 1)
            dst = (cqT[0][:, ft, :] if ft < 4 else ckvT[0][:, ft - 4, :])
            bank = ft
            act.activation(dst, ps[:, bank, :], ACT.Copy, scale=VT[:, V_QG + ft:V_QG + ft + 1]
                           ).then_inc(low_hi, 1)
        for i in range(4):
            mla_split(0, i)

        def softmax_exp(p, i):
            act.wait_ge(a_max, 8 * p + i + 1)
            act.activation(pr[:, i // 4, i % 4, :], ps[:, i, :], ACT.Exp, scale=float(QK) ** -0.5,
                           bias=nms[:, i:i + 1], accum_out=den[:, i:i + 1]).then_inc(a_exp, 1)

        def probT_hi(p, i):
            act.wait_ge(a_PT, 8 * p + i + 1)
            if i == 4:
                act.wait_ge(a_PV, 2 * p + 1)
            act.activation(pT[0][:, :, (i % 4) * P:(i % 4 + 1) * P],
                           ps[:, i, :].rearrange("p (j n) -> p j n", j=TT), ACT.Copy).then_inc(a_PThi, 1)

        def out_hi(p, h):
            act.wait_ge(a_PV, 2 * p + h + 1)
            act.activation(one(mixA[0], 2 * p + h), ps[:, 4 * h, :], ACT.Copy).then_inc(a_ohi, 1)

        def mla_pair(p, last):
            act.wait_ge(blk_done, N_MLA + 4 * p + 2)
            for t in range(TT):
                for h in range(2):
                    act.activation(pr[:, 0, t, h * QK:(h + 1) * QK], ps[:, t, h * QK:(h + 1) * QK], ACT.Square,
                                   accum_out=ssq[:, 2 * t + h:2 * t + h + 1]).then_inc(a_sq, 1)
            act.wait_ge(blk_done, N_MLA + 4 * p + 4)
            for t in range(TT):
                for h in range(2):
                    act.activation(pr[:, 1, t, h * 256:h * 256 + NOPE], ps[:, 4 + t, h * 256:h * 256 + NOPE],
                                   ACT.Square, accum_out=ssq[:, 8 + 2 * t + h:9 + 2 * t + h]).then_inc(a_sq, 1)
            act.activation(vv[0][:, :, :, :],
                           ps[:, 4:8, :].rearrange("p t (h e) -> p t h e", h=2)[:, :, :, NOPE:],
                           ACT.Copy).then_inc(a_vhi, 1)
            if not last:
                for i in range(4):
                    mla_split(p + 1, i)
            else:
                for i in range(3):
                    split_hi(act, N_OUT + i, i, N_OUT // RING + 1)
            for which, dst in enumerate((qT, kT)):
                act.wait_ge(a_T, 2 * p + which + 1)
                act.activation(dst[0][:, :, :], ps[:, 4 * which:4 * which + 3, :], ACT.Copy
                               ).then_inc(a_Thi, 1)
            for i in range(8):
                softmax_exp(p, i)
                if i >= 3:
                    probT_hi(p, i - 3)
                if i == 7:
                    out_hi(p, 0)
            for i in range(5, 8):
                probT_hi(p, i)
            out_hi(p, 1)
        with act.Fori(0, PAIRS - 1) as p:
            mla_pair(p, False)
        mla_pair(PAIRS - 1, True)

        for d in range(2):
            act.wait_ge(g_bias, 4 + d + 1)
            act.activation(gw[:, d, :], gw[:, d, :], ACT.Exp, scale=-1.0).then_inc(g_exp, 1)
        for d in range(2):
            act.wait_ge(g_exp, d + 1)
            act.activation(gw[:, d, :], gw[:, d, :], ACT.Ln, bias=1.0).then_inc(g_ln, 1)
        act.wait_ge(g_rows, 1)
        act.activation(gT[:, 2:4, :], gw[:, 2:4, :], ACT.Exp, scale=-1.0).then_inc(g_em, 1)

        with act.Fori(0, HM) as h:
            act.wait_ge(g_cols, 1)
            act.wait_ge(m_mask, 2 * (h + 1))
            for t in range(TT):
                if t >= 2:
                    act.wait_ge(m_S, 2 * TT * h + 2 * (t - 1))
                wf = (t + 1) * P
                for d in range(2):
                    bias = gcol[:, 0, d, t, bass.ds(h, 1)]
                    dg = slice(t * P, (t + 1) * P)
                    base = 0 if d == 0 else wf
                    off = slice(0, t * P) if d == 0 else slice((t + 1) * P, S)
                    dst_dg = et[:, t % 2, base + t * P:base + (t + 1) * P] if d == 0 \
                        else et[:, t % 2, base:base + P]
                    dst_off = et[:, t % 2, 0:t * P] if d == 0 else et[:, t % 2, base + P:base + S - t * P]
                    if off.stop > off.start:
                        act.activation(dst_off, gb[:, d, off], ACT.Exp, bias=bias).then_inc(m_exp, 1)
                    else:
                        act.activation(dst_dg, gbm[:, d, dg], ACT.Exp, bias=bias).then_inc(m_exp, 1)
                        continue
                    act.activation(dst_dg, gbm[:, d, dg], ACT.Exp, bias=bias).then_inc(m_exp, 1)
            act.wait_ge(m_rd, h + 1)
            for t in range(TT):
                wf = (t + 1) * P
                act.activation(sf[:, t, 0:wf], sf[:, t, 0:wf], ACT.Copy, scale=mrd[:, 0, t:t + 1]
                               ).then_inc(m_sc, 1)
                if wf < S:
                    act.activation(sf[:, t, wf:S], sbw[:, t, wf:S], ACT.Copy, scale=mrd[:, 1, t:t + 1]
                                   ).then_inc(m_sc, 1)
            for t in range(TT):
                act.wait_ge(m_WT, TT * h + t + 1)
                act.activation(wT[0][:, :, t * P:(t + 1) * P],
                               ps[:, 4 + t, :].rearrange("p (j n) -> p j n", j=TT), ACT.Copy
                               ).then_inc(m_WThi, 1)
            for v in range(2):
                act.wait_ge(m_V, 2 * h + v + 1)
                act.activation(msq[:, v, :], ps[:, 4 + v, :], ACT.Square).then_inc(m_sq, 1)
            for v in range(2):
                act.wait_ge(m_t2, 2 * h + v + 1)
                act.activation(one(mixM[0], 2 * h + v), sf[:, v, :], ACT.Copy).then_inc(m_ohi, 1)

        def out_step(g, b):
            n = N_OUT + GB * g + b + 3
            split_hi(act, n, (b + 3) % RING, N_OUT // RING + 2 * g + (b + 3) // RING + 1)

        for b in range(GB):
            out_step(0, b)
        with act.Fori(1, G_OUT) as g:
            for b in range(GB):
                out_step(g, b)
                if b == 0:
                    for i in range(4):
                        T = 4 * (g - 1) + i
                        act.wait_ge(x1_done, T + 1)
                        if i >= 2:
                            act.wait_ge(o_sqadd, T - 1)
                        else:
                            act.wait_ge(o_sqadd, 4 * (g - 1))
                        act.activation(sq2[:, i % 2, :], one(x1T, T), ACT.Square).then_inc(o_sq, 1)
        for i in range(4):
            T = 4 * (G_OUT - 1) + i
            act.wait_ge(x1_done, T + 1)
            act.wait_ge(o_sqadd, T - 1)
            act.activation(sq2[:, i % 2, :], x1T[:, T, :], ACT.Square).then_inc(o_sq, 1)
        for k in range(KT):
            act.wait_ge(u2_done, k + 1)
            act.activation(h2T[0][:, k, :], utmp2[:, k % 2, :], ACT.Identity,
                           bias=M[:, M_SH2 + k:M_SH2 + k + 1]).then_inc(h2_hi, 1)

        def ff_chunk(ch, last):
            for s in range(CB):
                if not (last and s + 3 >= CB):
                    split_hi(act, N_FF + CB * ch + s + 3, (s + 3) % RING,
                             N_FF // RING + CB // RING * ch + (s + 3) // RING + 1)
                if s in (GB, 2 * GB):
                    q = s // GB - 1
                    act.wait_ge(blk_done, N_FF + CB * ch + s)
                    T0 = CT * ch + 4 * q
                    for i in range(5):
                        if i < 4:
                            act.wait_ge(f_sq, T0 + max(i - 1, 0))
                            act.activation(utmp2[:, i % 2, :], ps[:, 4 * q + i, :], ACT.Relu
                                           ).then_inc(f_relu, 1)
                        if i >= 1:
                            act.wait_ge(f_sq, T0 + i)
                            act.activation(aT[0][:, 4 * q + i - 1, :], sq2[:, (i - 1) % 2, :], ACT.Copy
                                           ).then_inc(f_hi, 1)
        with act.Fori(0, CHUNKS - 1) as ch:
            ff_chunk(ch, False)
        ff_chunk(CHUNKS - 1, True)
        for t in range(TT):
            if t >= 2:
                act.wait_ge(y_stored[t % 2], 16)
            for k in range(0, 4, 2):
                act.wait_ge(y_T, 4 * t + k + 1)
                act.activation(yst[:, t % 2, 512 * k:512 * k + 512], ps[:, 4 * (t % 2) + k, :], ACT.Copy
                               ).then_inc(y_act, 1)

    @block.vector
    def _(dve):
        chain = [0]

        def link(ins):
            chain[0] += 1
            ins.then_inc(dve_step, 1)

        def sync():
            dve.wait_ge(dve_step, chain[0])

        dve.wait_ge(vec_loaded, 16 * 13)
        dve.tensor_copy(posf[:, :], posi[:, :]).then_inc(pos_f, 1)
        dve.wait_ge(vec_T, 1)
        dve.tensor_copy(VT[:, :], ps[:, 7, 0:V_ALL]).then_inc(vec_cols, 1)
        dve.wait_ge(vec_cols, 1)
        dve.wait_ge(silc_done, 1)

        def ada_units(pair, parity, us):
            for u2 in us:
                for kk in range(2):
                    for w in range(2):
                        i = 4 * u2 + 2 * kk + w
                        kt = 2 * u2 + kk
                        unit = 2 * u2 + w
                        if kk == 0:
                            dve.wait_ge(ada_loaded[unit % 4], 16 * (4 * pair + unit // 4 + 1))
                        src = araw[:, unit % 4, kk, :]
                        dst = acc[:, 2 * parity + w, :]
                        if kt == 0:
                            if not (isinstance(pair, int) and pair < 2):
                                dve.wait_ge(ada_summed, pair - 1)
                            dve.tensor_scalar(dst, src, silc[:, kt:kt + 1], None, ALU.mult).then_inc(ada_step, 1)
                        else:
                            dve.wait_ge(ada_step, 32 * pair + i - 1)
                            dve.scalar_tensor_tensor(dst, src, silc[:, kt:kt + 1], dst, ALU.mult, ALU.add
                                                     ).then_inc(ada_step, 1)

        def ada_cols(pair, bank, m0, m1):
            dve.wait_ge(ada_summed, pair + 1)
            for w, m in enumerate((m0, m1)):
                dve.tensor_tensor(M[:, bass.ds(m, 4)], ps[:, bank, 4 * w:4 * w + 4],
                                  VT[:, bass.ds(V_ADA + m, 4)], ALU.add).then_inc(ada_read, 1)

        def modulate(ks, src, gain, rst, tmp, dst, shift, s_u, s_hi, s_lo):
            for k in list(ks) + [None]:
                if k is not None:
                    if k >= 2:
                        dve.wait_ge(s_lo, k - 1)
                    dve.scalar_tensor_tensor(tmp[:, k % 2, :], src[:, k, :], gain[:, k:k + 1], rst[:, :],
                                             ALU.mult, ALU.mult).then_inc(s_u, 1)
                j = ks[-1] if k is None else k - 1
                if j >= ks[0]:
                    dve.wait_ge(s_hi, j + 1)
                    dve.scalar_tensor_tensor(dst[1][:, j, :], tmp[:, j % 2, :],
                                             M[:, shift + j:shift + j + 1], dst[0][:, j, :].bitcast(F),
                                             ALU.add, ALU.subtract).then_inc(s_lo, 1)

        for q in range(4):
            ada_units(q, q % 2, range(8))
            if q == 0:
                dve.wait_ge(ssq_bc, 1)
                dve.tensor_scalar(utmp[:, 0, :], ps[:, 4, :], 1.0 / D, EPS, ALU.mult, ALU.add
                                  ).then_inc(ms_done, 1)
            ada_cols(q, 5, M_SH1 + 4 * q, M_SC1 + 4 * q)
            dve.wait_ge(ada_read, 2 * (q + 1))
            link(dve.scalar_tensor_tensor(A1[:, 4 * q:4 * q + 4], M[:, M_SC1 + 4 * q:M_SC1 + 4 * q + 4], 1.0,
                                          VT[:, V_GMIX + 4 * q:V_GMIX + 4 * q + 4], ALU.add, ALU.mult))
            sync()
            if q == 0:
                dve.wait_ge(rstd_done, 1)
            dve.wait_ge(x_evac, 4 * TT)
            modulate(range(4 * q, 4 * q + 4), xT, A1, rstd, utmp, hT, M_SH1, u_done, h_hi, h_lo)

        dve.wait_ge(h_lo, KT)
        ada_units(4, 0, range(2))
        dve.wait_ge(xT_stored, 16)
        link(dve.tensor_tensor(ang[:, 0, :, :], VT[:, V_POS:V_POS + TT, None].to_broadcast([P, TT, ROPE // 2]),
                               freq[:, None, :].to_broadcast([P, TT, ROPE // 2]), ALU.mult))
        sync()
        big = 12582912.0
        two_pi = 2 * np.pi
        c1 = 6.28125
        c2 = float(np.float32(np.round((two_pi - c1) * 2 ** 20) / 2 ** 20))
        c3 = float(two_pi - c1 - c2)

        def step(ins):
            link(ins)
            sync()
        a = lambda i: ang[:, i, :, :]
        step(dve.tensor_scalar(a(1), a(0), float(1 / two_pi), big, ALU.mult, ALU.add))
        step(dve.tensor_scalar(a(1), a(1), big, None, ALU.subtract))
        step(dve.tensor_scalar(a(2), a(1), 1.0 / 2048, big, ALU.mult, ALU.add))
        step(dve.tensor_scalar(a(2), a(2), big, 2048.0, ALU.subtract, ALU.mult))
        step(dve.tensor_tensor(a(3), a(1), a(2), ALU.subtract))
        for cc in (c1, c2):
            for kk in (2, 3):
                step(dve.scalar_tensor_tensor(a(0), a(kk), -cc, a(0), ALU.mult, ALU.add))
        step(dve.scalar_tensor_tensor(a(0), a(1), -c3, a(0), ALU.mult, ALU.add))
        pi = float(np.float32(3.1415925))
        step(dve.tensor_scalar(a(4), a(0), pi, -pi, ALU.min, ALU.max))
        step(dve.tensor_scalar(a(1), a(0), float(np.pi / 2), None, ALU.add))
        step(dve.tensor_scalar(a(2), a(1), pi, -float(two_pi), ALU.is_gt, ALU.mult))
        step(dve.tensor_tensor(a(1), a(1), a(2), ALU.add))
        dve.tensor_scalar(a(5), a(1), pi, -pi, ALU.min, ALU.max).then_inc(ang_r, 1)
        ada_units(4, 0, range(2, 8))

        def in_steps(g, parity, piece):
            for b in range(GB):
                piece(b)
                if ada_on[0]:
                    ada_units(g + 3, parity, [b])
                if b == 6:
                    m = M_G1 + 8 * (g - 2)
                    ada_cols(g + 2, 4 * parity_half(parity) + 3, m, m + 4)
        ada_on = [True]

        def parity_half(parity):
            return parity

        def low_piece(b):
            if b == 6:
                dve.wait_ge(low_sq, 12)
                link(dve.tensor_scalar(ssq[:, 0:4], ssq[:, 0:4], 1.0 / QL, EPS, ALU.mult, ALU.add))
                dve.tensor_scalar(ssq[:, 4:8], ssq[:, 4:8], 1.0 / KVL, EPS, ALU.mult, ALU.add
                                  ).then_inc(low_ms, 1)
                link(dve.tensor_tensor(ckv[:, :, 256:320], ckv[:, :, 256:320],
                                       kg[:, None, NOPE:QK].to_broadcast([P, TT, ROPE]), ALU.mult))
                sync()
                dve.wait_ge(trig, 2)
                x1, x2 = ckv[:, :, 256:288], ckv[:, :, 288:320]
                tmp = [ang[:, i, :, :] for i in range(4)]
                link(dve.tensor_tensor(tmp[0], x1, cosT[:, :, :], ALU.mult))
                link(dve.tensor_tensor(tmp[1], x2, sinT[:, :, :], ALU.mult))
                link(dve.tensor_tensor(tmp[2], x1, sinT[:, :, :], ALU.mult))
                link(dve.tensor_tensor(tmp[3], x2, cosT[:, :, :], ALU.mult))
                sync()
                link(dve.tensor_tensor(rp[:, :, 0:32], tmp[0], tmp[1], ALU.subtract))
                link(dve.tensor_tensor(rp[:, :, 32:64], tmp[2], tmp[3], ALU.add))
            if b == 7:
                dve.wait_ge(low_rs, 1)
                for t in range(TT):
                    dve.tensor_scalar(cq[:, t, :], cq[:, t, :], rs[:, t:t + 1], None, ALU.mult
                                      ).then_inc(low_norm, 1)
                    dve.tensor_scalar(ckv[:, t, 0:256], ckv[:, t, 0:256], rs[:, 4 + t:5 + t], None, ALU.mult
                                      ).then_inc(low_norm, 1)

        in_steps(2, 1, low_piece)

        def conv_piece(g, half, gp):
            T0 = 4 * (g - 3)

            def piece(b):
                if b < 4:
                    y, p = yc[:, b % 2, :], ps[:, 4 * half + b, :]
                    dve.wait_ge(c_mid, T0 + b + 1)
                    for j, (tap, dst, src) in enumerate((
                            (0, slice(2, S), slice(0, S - 2)), (1, slice(1, S), slice(0, S - 1)),
                            (3, slice(0, S - 1), slice(1, S)), (4, slice(0, S - 2), slice(2, S)))):
                        ins = dve.scalar_tensor_tensor(y[:, dst], p[:, src], col(VT, V_CW + 16 * tap + T0 + b),
                                                       y[:, dst], ALU.mult, ALU.add)
                        if j < 3:
                            ins.then_inc(tap_step, 1)
                            dve.wait_ge(tap_step, 3 * (T0 + b) + j + 1)
                        else:
                            ins.then_inc(bank_free[half], 1)
                if 1 <= b <= 4:
                    i = b - 1
                    dve.wait_ge(c_hi, T0 + i + 1)
                    dve.tensor_tensor(stl[:, i % 2, :].bitcast(R), yc[:, i % 2, :], sth[:, i % 2, :],
                                      ALU.subtract).then_inc(c_lo, 1)
            return piece
        with dve.Fori(1, 3) as gp:
            in_steps(2 * gp + 1, 0, conv_piece(2 * gp + 1, 0, gp))
            in_steps(2 * gp + 2, 1, conv_piece(2 * gp + 2, 1, gp))

        def v_piece(g, half):
            T0 = 4 * (g - 3)

            def piece(b):
                if b < 4:
                    dve.wait_ge(c_hi, T0 + b + 1)
                    dve.tensor_tensor(stl[:, b % 2, :].bitcast(R), ps[:, 4 * half + b, :], sth[:, b % 2, :],
                                      ALU.subtract).then_inc(c_lo, 1)
                if b == 4:
                    dve.wait_ge(c_lo, T0 + 4)
                    dve.sem_inc(bank_free[half], 4)
            return piece
        in_steps(7, 0, v_piece(7, 0))
        in_steps(8, 1, v_piece(8, 1))
        ada_on[0] = False
        in_steps(9, 0, lambda b: None)

        for ft in range(6):
            dst, hi = ((cqT[1][:, ft, :], cqT[0][:, ft, :]) if ft < 4
                       else (ckvT[1][:, ft - 4, :], ckvT[0][:, ft - 4, :]))
            dve.wait_ge(low_hi, ft + 1)
            dve.scalar_tensor_tensor(dst, ps[:, ft, :], VT[:, V_QG + ft:V_QG + ft + 1], hi.bitcast(F),
                                     ALU.mult, ALU.subtract).then_inc(low_lo, 1)

        A_LINKS = 31
        with dve.Fori(0, PAIRS) as p:
            base = chain[0]
            cnt = [0]

            def alink(ins):
                cnt[0] += 1
                ins.then_inc(dve_step, 1)

            def async_():
                dve.wait_ge(dve_step, base + A_LINKS * p + cnt[0])
            dve.wait_ge(a_sq, 16 * (p + 1))
            alink(dve.tensor_tensor(ssq[:, 8:16].rearrange("p (t h) -> p t h", h=2),
                                    ssq[:, 8:16].rearrange("p (t h) -> p t h", h=2),
                                    pess[:, :, None].to_broadcast([P, TT, 2]), ALU.add))
            async_()
            dve.tensor_scalar(ssq[:, :], ssq[:, :], 1.0 / QK, EPS, ALU.mult, ALU.add).then_inc(a_ms, 1)
            dve.wait_ge(a_vhi, p + 1)
            alink(dve.tensor_tensor(vv[1][:, :, :, :],
                                    ps[:, 4:8, :].rearrange("p t (h e) -> p t h e", h=2)[:, :, :, NOPE:],
                                    vv[0][:, :, :, :].bitcast(F), ALU.subtract))
            dve.wait_ge(a_rs, p + 1)
            for t in range(TT):
                for h in range(2):
                    alink(dve.scalar_tensor_tensor(qn[:, t, h, :], ps[:, t, h * QK:(h + 1) * QK],
                                                   rs[:, 2 * t + h:2 * t + h + 1], qg[:, :],
                                                   ALU.mult, ALU.mult))
            async_()
            x1, x2 = qn[:, :, :, NOPE:NOPE + 32], qn[:, :, :, NOPE + 32:QK]
            cb = cosT[:, :, None, :].to_broadcast([P, TT, 2, 32])
            sb_ = sinT[:, :, None, :].to_broadcast([P, TT, 2, 32])
            alink(dve.tensor_tensor(rt[:, 0], x1, cb, ALU.mult))
            alink(dve.tensor_tensor(rt[:, 1], x2, sb_, ALU.mult))
            alink(dve.tensor_tensor(rt[:, 2], x1, sb_, ALU.mult))
            alink(dve.tensor_tensor(rt[:, 3], x2, cb, ALU.mult))
            async_()
            alink(dve.tensor_tensor(qr[:, :, :, 0:32], rt[:, 0], rt[:, 1], ALU.subtract))
            dve.tensor_tensor(qr[:, :, :, 32:64], rt[:, 2], rt[:, 3], ALU.add).then_inc(a_norm, 1)
            for t in range(TT):
                for h in range(2):
                    alink(dve.scalar_tensor_tensor(kn[:, t, h, :], ps[:, 4 + t, h * 256:h * 256 + NOPE],
                                                   rs[:, 8 + 2 * t + h:9 + 2 * t + h], kg[:, 0:NOPE],
                                                   ALU.mult, ALU.mult))
            (dve.tensor_tensor(kr[:, :, :, :], rp[:, :, None, :].to_broadcast([P, TT, 2, ROPE]),
                                    rs[:, 8:16].rearrange("p (t h) -> p t h", h=2)[:, :, :, None]
                                    .to_broadcast([P, TT, 2, ROPE]), ALU.mult)).then_inc(a_norm, 1)
            for which, dst in enumerate((qT, kT)):
                dve.wait_ge(a_Thi, 2 * p + which + 1)
                dve.tensor_tensor(dst[1][:, :, :], ps[:, 4 * which:4 * which + 3, :],
                                  dst[0][:, :, :].bitcast(F), ALU.subtract).then_inc(a_Tlo, 1)

            def rowmax(i):
                dve.wait_ge(a_S, 8 * p + i + 1)
                alink(dve.reduce_max(nmax[:, i:i + 1], ps[:, i, :], AX.X))
                async_()
                dve.tensor_scalar(nms[:, i:i + 1], nmax[:, i:i + 1], -float(QK) ** -0.5, None, ALU.mult
                                  ).then_inc(a_max, 1)

            def prob(i):
                dve.wait_ge(a_exp, 8 * p + i + 1)
                dve.reciprocal(rden[:, i:i + 1], den[:, i:i + 1]).then_inc(dve_r, 1)
                dve.wait_ge(dve_r, 8 * p + i + 1)
                dve.tensor_scalar(pr[:, i // 4, i % 4, :], pr[:, i // 4, i % 4, :], rden[:, i:i + 1], None,
                                  ALU.mult).then_inc(a_prob, 1)

            def probT_lo(i):
                dve.wait_ge(a_PThi, 8 * p + i + 1)
                q = slice((i % 4) * P, (i % 4 + 1) * P)
                dve.tensor_tensor(pT[1][:, :, q], ps[:, i, :].rearrange("p (j n) -> p j n", j=TT),
                                  pT[0][:, :, q].bitcast(F), ALU.subtract).then_inc(a_PTlo, 1)

            def out_lo(h):
                dve.wait_ge(a_ohi, 2 * p + h + 1)
                dve.tensor_tensor(one(mixA[1], 2 * p + h), ps[:, 4 * h, :],
                                  one(mixA[0], 2 * p + h).bitcast(F), ALU.subtract).then_inc(a_olo, 1)
            for i in range(8):
                rowmax(i)
                if i >= 2:
                    prob(i - 2)
                if i >= 4:
                    probT_lo(i - 4)
            prob(6)
            prob(7)
            out_lo(0)
            for i in range(4, 8):
                probT_lo(i)
            out_lo(1)
            assert cnt[0] == A_LINKS, cnt[0]
        chain[0] += A_LINKS * PAIRS

        dve.wait_ge(g_T, 1)
        for k in range(4):
            dve.tensor_scalar(gT[:, k, :], ps[0:HM, k, :], bgate[:, k:k + 1], None, ALU.add
                              ).then_inc(g_bias, 1)
        dve.wait_ge(g_bias, 4)
        for d in range(2):
            f = gT[:, 2 * d + 1, :]
            dve.scalar_tensor_tensor(gw[:, d, :], f, -1.0, f, ALU.mult, ALU.max).then_inc(g_bias, 1)
        dve.wait_ge(g_ln, 2)
        fwd, bwd = slice(None), slice(None, None, -1)
        for d in range(2):
            f = gT[:, 2 * d + 1, :]
            link(dve.scalar_tensor_tensor(gw[:, d, :], f, 0.0, gw[:, d, :], ALU.min, ALU.subtract))
        sync()
        for d, way in enumerate((fwd, bwd)):
            link(dve.tensor_tensor_scan(gw[:, 2 + d, way], gw[:, d, way], gw[:, d, way], 0.0,
                                        ALU.add, ALU.bypass))
        sync()
        for d in range(2):
            link(dve.tensor_tensor(grw[:, d, :], gT[:, 2 * d, :], gw[:, 2 + d, :], ALU.subtract))
        sync()
        for d, way in enumerate((fwd, bwd)):
            link(dve.tensor_tensor_scan(gw[:, d, way], grw[:, d, way], grw[:, d, way], -3.0e38,
                                        ALU.max, ALU.bypass))
        sync()
        link(dve.tensor_tensor(gw[:, 2:4, :], gw[:, 2:4, :], gw[:, 0:2, :], ALU.add))
        link(dve.tensor_scalar(gT[:, 0:2, :], gw[:, 0:2, :], -1.0, None, ALU.mult))
        sync()
        dve.sem_inc(g_rows, 1)
        dve.wait_ge(g_colT, 1)
        dve.tensor_copy(gcol[:, :, :, :, :].rearrange("p w d t h -> p (w d t h)"), ps[:, 7, 0:64]
                        ).then_inc(g_cols, 1)

        NEXP = 14

        H_LINKS = 4
        with dve.Fori(0, HM) as h:
            hb = chain[0]
            cnt = [0]

            def hlink(ins):
                cnt[0] += 1
                ins.then_inc(dve_step, 1)

            def hsync():
                dve.wait_ge(dve_step, hb + H_LINKS * h + cnt[0])
            done = 0
            for t in range(TT):
                wf = (t + 1) * P
                done += (1 if t == 0 else 2) + (1 if t == TT - 1 else 2)
                dve.wait_ge(m_exp, NEXP * h + done)
                dve.wait_ge(m_QK, TT * h + t + 1)
                dve.tensor_tensor_reduce(sf[:, t, 0:wf], ps[:, t, 0:wf], et[:, t % 2, 0:wf], DM ** -0.5, 0.0,
                                         ALU.mult, ALU.add, mden[:, 0, t:t + 1]).then_inc(m_S, 1)
                dve.tensor_tensor_reduce(sbw[:, t, t * P:S], ps[:, t, t * P:S], et[:, t % 2, wf:wf + S - t * P],
                                         DM ** -0.5, 0.0, ALU.mult, ALU.add, mden[:, 1, t:t + 1]
                                         ).then_inc(m_S, 1)
            dve.wait_ge(m_S, 2 * TT * (h + 1))
            hlink(dve.scalar_tensor_tensor(mden2[:, :, :], mden[:, :, :], -1.0, mden[:, :, :],
                                           ALU.mult, ALU.max))
            hsync()
            hlink(dve.tensor_tensor(mden2[:, :, :], mden2[:, :, :],
                                    gcol[:, 1, :, :, bass.ds(h, 1)].rearrange("p d t a -> p d (t a)"), ALU.max))
            hsync()
            dve.reciprocal(mrd[:, :, :], mden2[:, :, :]).then_inc(m_rd, 1)
            dve.wait_ge(m_rd, h + 1)
            sc = 0
            for t in range(TT):
                sc += 2 if t < TT - 1 else 1
                dve.wait_ge(m_sc, 7 * h + sc)
                dg = slice(t * P, (t + 1) * P)
                dve.scalar_tensor_tensor(sf[:, t, dg], sbw[:, t, dg], mrd[:, 1, t:t + 1], sf[:, t, dg],
                                         ALU.mult, ALU.add).then_inc(m_w, 1)
            for t in range(TT):
                q = slice(t * P, (t + 1) * P)
                dve.wait_ge(m_WThi, TT * h + t + 1)
                dve.tensor_tensor(wT[1][:, :, q], ps[:, 4 + t, :].rearrange("p (j n) -> p j n", j=TT),
                                  wT[0][:, :, q].bitcast(F), ALU.subtract).then_inc(m_WTlo, 1)
            dve.wait_ge(m_ss, h + 1)
            dve.tensor_scalar(et[:, 0, 0:S], ps[:, 6, :], 1.0 / DM, EPS, ALU.mult, ALU.add).then_inc(m_ms, 1)
            dve.wait_ge(m_rs, h + 1)
            for v in range(2):
                hlink(dve.scalar_tensor_tensor(sf[:, v, :], ps[:, 4 + v, :], col(VT, V_MG + 2 * h + v),
                                               et[:, 0, 0:S], ALU.mult, ALU.mult))
            hsync()
            dve.wait_ge(m_v_in, 48 * (h + 1))
            for v in range(2):
                dve.tensor_tensor(sf[:, v, :], sf[:, v, :], mo[:, v, :], ALU.mult).then_inc(m_t2, 1)
            for v in range(2):
                dve.wait_ge(m_ohi, 2 * h + v + 1)
                dve.tensor_tensor(one(mixM[1], 2 * h + v), sf[:, v, :], one(mixM[0], 2 * h + v).bitcast(F),
                                  ALU.subtract).then_inc(m_olo, 1)
            assert cnt[0] == H_LINKS
        chain[0] += H_LINKS * HM

        dve.wait_ge(xT_back, 16)
        dve.wait_ge(ada_read, 24)

        def residual(gp, half):
            g = 2 * gp + half
            dve.wait_ge(blk_done, N_OUT + GB * g + GB)
            for i in range(4):
                T = 4 * g + i
                dve.scalar_tensor_tensor(one(x1T, T), ps[:, 4 * half + i, :], col(M, M_G1 + T), one(x1T, T),
                                         ALU.mult, ALU.add).then_inc(x1_done, 1)
            dve.wait_ge(x1_done, 4 * g + 4)
            dve.sem_inc(o_free[half], 4)
            for i in range(4):
                T = 4 * g + i
                dve.wait_ge(o_sq, T + 1)
                dve.wait_ge(o_sqadd, T + 0)
                dve.tensor_tensor(sqacc2[:, :], sqacc2[:, :], sq2[:, i % 2, :], ALU.add).then_inc(o_sqadd, 1)
        dve.memset(sqacc2[:, :], 0.0).then_inc(sq_zero, 1)
        dve.wait_ge(sq_zero, 1)
        with dve.Fori(0, G_OUT // 2) as gp:
            residual(gp, 0)
            residual(gp, 1)
        dve.wait_ge(o_ss, 1)
        dve.tensor_scalar(utmp2[:, 0, :], ps[:, 0, :], 1.0 / D, EPS, ALU.mult, ALU.add).then_inc(o_ms, 1)
        link(dve.scalar_tensor_tensor(A1[:, :], M[:, M_SC2:M_SC2 + KT], 1.0, VT[:, V_GMLP:V_GMLP + KT],
                                      ALU.add, ALU.mult))
        dve.wait_ge(o_rs, 1)
        sync()
        modulate(range(KT), x1T, A1, rstd2, utmp2, h2T, M_SH2, u2_done, h2_hi, h2_lo)

        with dve.Fori(0, CHUNKS) as ch:
            for q in range(2):
                T0 = CT * ch + 4 * q
                for i in range(5):
                    if i < 4:
                        dve.wait_ge(f_relu, T0 + i + 1)
                        dve.wait_ge(f_lo, T0 + max(i - 1, 0))
                        dve.tensor_tensor(sq2[:, i % 2, :], utmp2[:, i % 2, :], utmp2[:, i % 2, :], ALU.mult
                                          ).then_inc(f_sq, 1)
                    if i >= 1:
                        dve.wait_ge(f_hi, T0 + i)
                        dve.tensor_tensor(aT[1][:, 4 * q + i - 1, :], sq2[:, (i - 1) % 2, :],
                                          aT[0][:, 4 * q + i - 1, :].bitcast(F), ALU.subtract
                                          ).then_inc(f_lo, 1)
                dve.sem_inc(f_free[q], 4)
            for q in range(4):
                dve.wait_ge(blk_done, N_FF + CB * ch + 2 * GB + 4 * q + 4)
                for i in range(4):
                    T = 4 * q + i
                    dve.scalar_tensor_tensor(x1T[:, T, :], ps[:, 4 * (q % 2) + i, :],
                                             M[:, M_G2 + T:M_G2 + T + 1], x1T[:, T, :], ALU.mult, ALU.add
                                             ).then_inc(f_free[q % 2], 1)
        for t in range(TT):
            if t >= 2:
                dve.wait_ge(y_stored[t % 2], 16)
            for k in range(1, 4, 2):
                dve.wait_ge(y_T, 4 * t + k + 1)
                dve.tensor_copy(yst[:, t % 2, 512 * k:512 * k + 512], ps[:, 4 * (t % 2) + k, :]
                                ).then_inc(y_dve, 1)

    perm.close()


_INS = ["x", "c", "positions", "w_ada", "b_ada", "norm_mix_g", "w_in", "b_gates", "conv_w", "conv_b",
        "q_lora_g", "w_uq", "kv_lora_g", "w_ukv", "q_norm_g", "k_norm_g", "mlstm_norm_g",
        "w_out", "norm_mlp_g", "w_ff1", "w_ff2"]
_FLAT = {"w_ada": 2, "w_in": 2, "w_uq": 2, "w_ukv": 2, "w_out": 2, "w_ff1": 2, "w_ff2": 2, "x": 2}


def program(nc, shapes):
    aps = []
    for name in _INS:
        shape, dt = shapes[name]
        ap = nc.dram_tensor(f"in_{name}", shape, dt, kind="ExternalInput").ap()
        if name in _FLAT:
            ap = ap.rearrange("a m n -> (a m) n")
        elif len(shape) == 3:
            ap = ap.rearrange("a m n -> (a m n)")
        else:
            ap = ap.rearrange("a n -> (a n)")
        aps.append(ap)
    out = nc.dram_tensor("out", (1, S, D), F, kind="ExternalOutput").ap()
    build(nc, *aps, out.rearrange("a s d -> (a s) d"))


def kernel(**inputs):
    import concourse.bacc as bacc
    from concourse.bass_utils import run_bass_kernel_spmd

    nc = bacc.Bacc("TRN2", target_bir_lowering=False, num_devices=1)
    arrays = {f"in_{n}": np.ascontiguousarray(inputs[n]) for n in _INS}
    program(nc, {n: (arrays[f"in_{n}"].shape, mybir.dt.from_np(arrays[f"in_{n}"].dtype)) for n in _INS})
    r = run_bass_kernel_spmd(nc, [arrays], core_ids=[0])
    return r.results[0]["out"]
```

```python
from contextlib import ExitStack

import numpy as np

import concourse.bass as bass
from concourse import mybir

F = mybir.dt.float32
R = mybir.dt.float32r
I32 = mybir.dt.int32
ALU = mybir.AluOpType
ACT = mybir.ActivationFunctionType
AX = mybir.AxisListType

P = 128
D = 2048
S = 512
KT = D // P
TT = S // P
NH, NOPE, ROPE, VD = 8, 128, 64, 128
QK = NOPE + ROPE
QL, KVL = 512, 256
HM, DM = 4, 256
MW = HM * DM
DFF = 4 * D
W1ROWS = 512 + 256 + 64
DIN = QL + KVL + ROPE + 4 * MW + 4 * HM
EPS = 1e-6
NEG = -3.0e38
KB = 2
RING = 4
GB = KT // KB

G_IN = 10
N_MLA = G_IN * GB
PAIRS = NH // 2
N_OUT = N_MLA + 4 * PAIRS
G_OUT = D // 512
N_FF = N_OUT + G_OUT * GB
CH = 1024
CHUNKS = DFF // CH
CT = CH // P
CB = CH // 512 * GB + G_OUT * (CT // KB)

V_C, V_GMIX, V_GMLP, V_CB, V_QG, V_KVG, V_MG = 0, 16, 32, 48, 64, 68, 70
V_ROWS = 78
V_ADA = V_ROWS
V_CW = V_ADA + 96
V_POS = V_CW + 80
V_ALL = V_POS + TT
M_SH1, M_SC1, M_G1, M_SH2, M_SC2, M_G2 = 0, 16, 32, 48, 64, 80


def rope_freqs():
    half = ROPE // 2
    return np.float32(10000.0) ** (-np.arange(half, dtype=np.float32) / np.float32(half))


def build(nc, x, c, positions, w_ada, b_ada, norm_mix_g, w_in, b_gates, conv_w, conv_b,
          q_lora_g, w_uq, kv_lora_g, w_ukv, q_norm_g, k_norm_g, mlstm_norm_g,
          w_out, norm_mlp_g, w_ff1, w_ff2, out):
    perm = ExitStack()

    def at(stack, name, shape, dt=F):
        return stack.enter_context(nc.sbuf_tensor(name, shape, dt))

    def sem(name):
        return perm.enter_context(nc.semaphore(name))

    xT_d = nc.dram_tensor("xT_d", (P, KT, S), F, kind="Internal").ap()
    qk_d = nc.dram_tensor("qk_d", (2, P, 2 * MW // P, S), F, kind="Internal").ap()
    v_d = nc.dram_tensor("v_d", (2, P, TT, MW), F, kind="Internal").ap()
    mix_d = nc.dram_tensor("mix_d", (P, KT, 2, S), F, kind="Internal").ap()
    o_d = nc.dram_tensor("o_d", (P, MW // P, S), F, kind="Internal").ap()
    g_d = nc.dram_tensor("g_d", (HM, 2, S), F, kind="Internal").ap()

    wraw = at(perm, "wraw", [P, RING, KB, 512])
    whi = at(perm, "whi", [P, RING, KB, 512], R)
    wlo = at(perm, "wlo", [P, RING, KB, 512], R)
    ident = at(perm, "ident", [P, P])
    ones = at(perm, "ones", [P, P])
    mask = at(perm, "mask", [P, 2, P])
    VT = at(perm, "VT", [P, V_ALL])
    M = at(perm, "M", [P, 96])
    silc = at(perm, "silc", [P, KT])
    A1 = at(perm, "A1", [P, KT])
    freq = at(perm, "freq", [P, ROPE // 2])
    cosT = at(perm, "cosT", [P, TT, ROPE // 2])
    sinT = at(perm, "sinT", [P, TT, ROPE // 2])
    qg = at(perm, "qg", [P, QK])
    kg = at(perm, "kg", [P, QK])
    bgate = at(perm, "bgate", [HM, 4])
    wgate = at(perm, "wgate", [P, KT, 16])
    rp = at(perm, "rp", [P, TT, ROPE])
    ssq = at(perm, "ssq", [P, 16])
    rs = at(perm, "rs", [P, 16])
    pess = at(perm, "pess", [P, TT])
    nhalf = at(perm, "nhalf", [P, 1])
    rc = at(perm, "rc", [P, 2, TT])
    gcol = at(perm, "gcol", [P, 2, 2, TT, HM])

    with ExitStack() as st:
        xnat = at(st, "xnat", [P, 2, D])
        rstd = at(st, "rstd", [P, S])
        utmp = at(st, "utmp", [P, 2, S])
        rows0 = at(st, "rows0", [V_ROWS, P])
        rows1 = at(st, "rows1", [96, P])
        rows2 = at(st, "rows2", [80, P])
        posi = at(st, "posi", [TT, P], I32)
        posf = at(st, "posf", [TT, P])
    low = ExitStack()
    cqT = [at(low, f"cqT{i}", [P, QL // P, S], R) for i in range(2)]
    with ExitStack() as st:
        cq = at(st, "cq", [P, TT, QL])
    ckvT = [at(low, f"ckvT{i}", [P, KVL // P, S], R) for i in range(2)]
    ckv = at(low, "ckv", [P, TT, 336])
    with ExitStack() as st:
        with ExitStack() as s2:
            xsq = at(s2, "xsq", [P, TT, D])
        hT = [at(st, f"hT{i}", [P, KT, S], R) for i in range(2)]
        araw = at(st, "araw", [P, 4, 2, 512])
        acc = at(st, "acc", [P, 4, 512])
        with ExitStack() as s2:
            xT = at(s2, "xT", [P, KT, S])
        with ExitStack() as s2:
            yc = at(s2, "yc", [P, 2, S])
            sth = at(s2, "sth", [P, 2, S])
            stl = at(s2, "stl", [P, 2, S])
            ang = at(s2, "ang", [P, 6, TT, ROPE // 2])
    with ExitStack() as st:
        qn = at(st, "qn", [P, TT, 2, QK])
        qr = at(st, "qr", [P, TT, 2, ROPE])
        kn = at(st, "kn", [P, TT, 2, NOPE])
        kr = at(st, "kr", [P, TT, 2, ROPE])
        rt = at(st, "rt", [P, 4, TT, 2, ROPE // 2])
        vraw = at(st, "vraw", [P, TT, 2, VD])
        vv = [at(st, f"vv{i}", [P, TT, 2, VD], R) for i in range(2)]
        qT = [at(st, f"qT{i}", [P, 3, S], R) for i in range(2)]
        kT = [at(st, f"kT{i}", [P, 3, S], R) for i in range(2)]
        ost = at(st, "ost", [P, 2, 2, S])
        pr = at(st, "pr", [P, TT, S])
        pT = [at(st, f"pT{i}", [P, TT, S], R) for i in range(2)]
        nmax = at(st, "nmax", [P, 8])
        nms = at(st, "nms", [P, 8])
        den = at(st, "den", [P, 8])
        rden = at(st, "rden", [P, 8])
    mixst = ExitStack()
    mixA = at(mixst, "mixA", [P, NH, 2, S], R)
    mixM = at(mixst, "mixM", [P, NH, 2, S], R)
    with ExitStack() as st:
        wT = [at(st, f"wT{i}", [P, TT, S], R) for i in range(2)]
        sf = at(st, "sf", [P, TT, S])
        sbw = at(st, "sbw", [P, TT, S])
        mo = at(st, "mo", [P, 2, S])
        mq = [at(st, f"mq{i}", [P, 2, S], R) for i in range(2)]
        mk = [at(st, f"mk{i}", [P, 2, S], R) for i in range(2)]
        mden = at(st, "mden", [P, 2, TT])
        mden2 = at(st, "mden2", [P, 2, TT])
        mrd = at(st, "mrd", [P, 2, TT])
    with ExitStack() as st:
        x1T = at(st, "x1T", [P, KT, S])
        with ExitStack() as s2:
            araw2 = at(s2, "araw2", [P, 4, 2, 512])
        ah0 = at(st, "ah", [P, CT, S], R)
    mixst.close()
    with ExitStack() as st:
        h2T = [at(st, f"h2T{i}", [P, KT, S], R) for i in range(2)]
    with ExitStack() as st:
        yst = at(st, "yst", [P, 2, D])
    low.close()
    with ExitStack() as st:
        mv = [at(st, f"mv{i}", [P, TT, DM], R) for i in range(2)]
        gb = at(st, "gb", [P, 2, S])
        gbm = at(st, "gbm", [P, 2, S])
        et = at(st, "et", [P, 2, 640])
        msq = at(st, "msq", [P, 2, S])
        mt = at(st, "mt", [P, 2, S])
    grows = araw[0:HM, :, :, :].rearrange("p a b n -> p (a b) n")
    gT, gw = grows[:, 0:4, :], grows[:, 4:8, :]
    grw = acc[0:HM, 0:2, :]
    with ExitStack() as st:
        with ExitStack() as s2:
            acc2 = at(s2, "acc2", [P, 4, 512])
        al0 = at(st, "al", [P, CT, S], R)
        sqacc2 = at(st, "sqacc2", [P, S])
        rstd2 = at(st, "rstd2", [P, S])
        utmp2 = at(st, "utmp2", [P, 2, S])
        sq2 = at(st, "sq2", [P, 2, S])
    aT = [ah0, al0]
    ps = perm.enter_context(nc.psum_tensor("ps", [P, 8, 512], F))

    def mix(part, kt):
        return (mixA if kt < NH else mixM)[:, kt % NH, part, :]

    WT_ORDER = (2, 3, 0, 1)

    w_loaded = [sem(f"w_loaded{i}") for i in range(RING)]
    hi_ready, lo_ready, blk_done = sem("hi_ready"), sem("lo_ready"), sem("blk_done")
    vec_loaded, gate_loaded = sem("vec_loaded"), sem("gate_loaded")
    const_done, vec_T, vec_cols = sem("const_done"), sem("vec_T"), sem("vec_cols")
    pos_f = sem("pos_f")
    silc_done = sem("silc_done")
    x_loaded = [sem("x_loaded0"), sem("x_loaded1")]
    x_T, x_evac, kv_part = sem("x_T"), sem("x_evac"), sem("kv_part")

    def norm_sems(name):
        return [sem(f"{name}_{x}") for x in ("sum", "mean", "pow", "diag", "bcast", "scale")]
    n1, n2, nm = norm_sems("norm1"), norm_sems("norm2"), norm_sems("head_norm")
    ada_loaded = [sem(f"ada_loaded{i}") for i in range(4)]
    ada_step, ada_summed, ada_read = sem("ada_step"), sem("ada_summed"), sem("ada_read")
    u_done, h_sum, h_hi, h_lo = sem("u_done"), sem("h_sum"), sem("h_hi"), sem("h_lo")
    xT_stored = sem("xT_stored")
    bank_free = [sem("bank_free0"), sem("bank_free1")]
    c_mid, c_silu, c_hi, c_lo = sem("c_mid"), sem("c_silu"), sem("c_hi"), sem("c_lo")
    staged = [sem("staged0"), sem("staged1")]
    o_stored = [sem(f"o_stored{i}") for i in range(4)]
    low_sq, low_ms, low_rs, low_norm = sem("low_sq"), sem("low_ms"), sem("low_rs"), sem("low_norm")
    low_T, low_hi, low_lo = sem("low_T"), sem("low_hi"), sem("low_lo")
    ang_r, trig = sem("ang_r"), sem("trig")
    dve_step, act_step, pool_step = sem("dve_step"), sem("act_step"), sem("pool_step")
    tap_step, sq_zero = sem("tap_step"), sem("sq_zero")
    a_qsq, a_ksq, a_qms, a_kms, a_qrs, a_krs = (sem("a_qsq"), sem("a_ksq"), sem("a_qms"), sem("a_kms"),
                                                sem("a_qrs"), sem("a_krs"))
    a_qn, a_qr, a_kn, a_vraw, a_vhi, a_vlo = (sem("a_qn"), sem("a_qr"), sem("a_kn"), sem("a_vraw"),
                                              sem("a_vhi"), sem("a_vlo"))
    a_Tq, a_Tk, a_qThi, a_qTlo, a_kThi, a_kTlo = (sem("a_Tq"), sem("a_Tk"), sem("a_qThi"), sem("a_qTlo"),
                                                  sem("a_kThi"), sem("a_kTlo"))
    a_S, a_max, a_exp, a_prob = sem("a_S"), sem("a_max"), sem("a_exp"), sem("a_prob")
    a_PT, a_PThi, a_PTlo, a_PV = sem("a_PT"), sem("a_PThi"), sem("a_PTlo"), sem("a_PV")
    a_ohi, a_olo = sem("a_ohi"), sem("a_olo")
    mix_stored = [sem("mix_stored0"), sem("mix_stored1")]
    mixA_in = sem("mixA_in")
    g_T, g_bias, g_exp, g_ln, g_rows, g_em = (sem("g_T"), sem("g_bias"), sem("g_exp"), sem("g_ln"),
                                              sem("g_rows"), sem("g_em"))
    g_stored, g_colT, g_cols = sem("g_stored"), sem("g_colT"), sem("g_cols")
    m_qk_in, m_v_in, m_g_in = sem("m_qk_in"), sem("m_v_in"), sem("m_g_in")
    m_mask, m_exp, m_S, m_sc, m_rd, m_w = (sem("m_mask"), sem("m_exp"), sem("m_S"), sem("m_sc"),
                                           sem("m_rd"), sem("m_w"))
    m_QK, m_WT, m_WThi, m_WTlo, m_V = sem("m_QK"), sem("m_WT"), sem("m_WThi"), sem("m_WTlo"), sem("m_V")
    m_normed = sem("m_normed")
    m_sq, m_t2, m_ohi, m_olo = sem("m_sq"), sem("m_t2"), sem("m_ohi"), sem("m_olo")
    xT_back, o_free, x1_done, o_sq, o_sqadd = (sem("xT_back"), [sem("o_free0"), sem("o_free1")],
                                               sem("x1_done"), sem("o_sq"), sem("o_sqadd"))
    u2_done, h2_hi, h2_lo = sem("u2_done"), sem("h2_hi"), sem("h2_lo")
    f_free = [sem("f_free0"), sem("f_free1")]
    f_relu, f_sq, f_hi, f_lo = sem("f_relu"), sem("f_sq"), sem("f_hi"), sem("f_lo")
    y_T, y_act, y_dve = sem("y_T"), sem("y_act"), sem("y_dve")
    y_stored = [sem("y_stored0"), sem("y_stored1")]

    w_in3 = w_in.rearrange("(k p) n -> p k n", p=P)
    w_ada3 = w_ada.rearrange("(k p) n -> p k n", p=P)
    w_uq3 = w_uq.rearrange("(k p) n -> p k n", p=P)
    w_ukv3 = w_ukv.rearrange("(k p) n -> p k n", p=P)
    w_out3 = w_out.rearrange("(k p) n -> p k n", p=P)
    w_ff13 = w_ff1.rearrange("(k p) n -> p k n", p=P)
    w_ff23 = w_ff2.rearrange("(k p) n -> p k n", p=P)

    def one(tile, i):
        return tile[:, bass.ds(i, 1), :].rearrange("p a n -> p (a n)")

    def col(tile, i):
        return tile[:, bass.ds(i, 1)]

    block = perm.enter_context(nc.Block())

    def first_block(n):
        return n % 4 // 2, 2 * (n // 4) + n % 2

    def load_block(sp, n, slot, src, cols=512, kb=KB, first=False):
        if not first:
            sp.wait_ge(lo_ready, n - RING + 1)
        sp.dma_start(wraw[:, slot, 0:kb, 0:cols], src).then_inc(w_loaded[slot], 16)

    def split_hi(act, n, slot, use, cols=512, kb=KB, first=False):
        act.wait_ge(w_loaded[slot], 16 * use)
        if not first:
            act.wait_ge(blk_done, n - RING + 1)
        act.activation(whi[:, slot, 0:kb, 0:cols], wraw[:, slot, 0:kb, 0:cols],
                       ACT.Copy).then_inc(hi_ready, 1)

    def split_lo(pool, n, slot, cols=512, kb=KB):
        pool.wait_ge(hi_ready, n + 1)
        pool.tensor_tensor(wlo[:, slot, 0:kb, 0:cols], wraw[:, slot, 0:kb, 0:cols],
                           whi[:, slot, 0:kb, 0:cols].bitcast(F), ALU.subtract).then_inc(lo_ready, 1)

    def ada_unit_release(pair, u):
        return 32 * pair + 4 * (u // 2) + 3 + u % 2

    def norm_sum(pe, sems, bank, squares):
        for t in range(TT):
            for i, sq in enumerate(squares):
                ins = pe.matmul(ps[:, bank, t:t + 1], sq[:, t * P:(t + 1) * P], ones[:, 0:1],
                                start=(i == 0), stop=(i == len(squares) - 1))
        ins.then_inc(sems[0], 1)

    def norm_mean(dve, sems, bank, width, at=0):
        dve.wait_ge(sems[0], at + 1)
        dve.tensor_scalar(rc[:, 0, :], ps[:, bank, 0:TT], 1.0 / width, EPS, ALU.mult, ALU.add
                          ).then_inc(sems[1], 1)

    def norm_pow(pool, sems, at=0):
        pool.wait_ge(sems[1], at + 1)
        pool.tensor_tensor(rc[:, 1, :], rc[:, 0, :], nhalf[:, 0:1].to_broadcast([P, TT]), ALU.pow
                           ).then_inc(sems[2], 1)

    def norm_diag(dve, sems, tile, at=0):
        dve.wait_ge(sems[2], at + 1)
        dve.tensor_tensor(tile.rearrange("p (t n) -> p t n", t=TT),
                          ident[:, None, :].to_broadcast([P, TT, P]),
                          rc[:, 1, :, None].to_broadcast([P, TT, P]), ALU.mult).then_inc(sems[3], 1)

    def norm_bcast(pe, sems, bank, tile, at=0):
        pe.wait_ge(sems[3], at + 1)
        pe.matmul(ps[:, bank, :], ones[:, :], tile, start=True, stop=True).then_inc(sems[4], 1)

    def norm_scale(act, sems, bank, tile, at=0):
        act.wait_ge(sems[4], at + 1)
        act.activation(tile, ps[:, bank, :], ACT.Copy).then_inc(sems[5], 1)

    @block.sync
    def _(sp):
        vr = lambda ap: ap.rearrange("(a p) -> a p", p=P)
        loads = [
            (rows0[V_C:V_C + 16, :], vr(c)), (rows0[V_GMIX:V_GMIX + 16, :], vr(norm_mix_g)),
            (rows0[V_GMLP:V_GMLP + 16, :], vr(norm_mlp_g)), (rows0[V_CB:V_CB + 16, :], vr(conv_b)),
            (rows0[V_QG:V_QG + 4, :], vr(q_lora_g)), (rows0[V_KVG:V_KVG + 2, :], vr(kv_lora_g)),
            (rows0[V_MG:V_MG + 8, :], vr(mlstm_norm_g)), (rows1[:, :], vr(b_ada)),
            (rows2[:, :], vr(conv_w)), (posi[:, :], vr(positions)),
            (qg[:, :], q_norm_g.partition_broadcast(P)), (kg[:, :], k_norm_g.partition_broadcast(P)),
            (bgate[:, :], b_gates.rearrange("(k h) -> h k", h=HM)),
        ]
        for dst, src in loads:
            sp.dma_start(dst, src, allow_slow_non_contiguous=dst.tensor.name == "bgate").then_inc(vec_loaded, 16)
        sp.dma_start(wgate[:, :, :], w_in3[:, :, DIN - 16:DIN]).then_inc(gate_loaded, 16)

        def ada_load(pair, u, col0, col1, first=False, raw=araw):
            if not first:
                if u >= 4:
                    sp.wait_ge(ada_step, ada_unit_release(pair, u - 4))
                else:
                    sp.wait_ge(ada_step, ada_unit_release(pair - 1, u + 12))
            k0 = 2 * (u // 2)
            sp.dma_start(raw[:, u % 4, :, :],
                         w_ada3[:, k0:k0 + 2, bass.ds((col0, col1)[u % 2], 512)]
                         ).then_inc(ada_loaded[u % 4], 16)

        for q in range(4):
            for u in range(16):
                ada_load(q, u, 512 * q, D + 512 * q, first=(q == 0 and u < 4))
                if u % 4 == 3:
                    n = 4 * q + u // 4
                    g, b = first_block(n)
                    cols = 320 if g == 1 else 512
                    load_block(sp, n, n % RING, w_in3[:, KB * b:KB * b + KB, 512 * g:512 * g + cols],
                               cols, first=(q == 0))
        def later_ada_load(pair, u, raw=araw):
            col0 = 2 * D + 1024 * (pair - 4)
            ada_load(pair, u, col0, col0 + 512, raw=raw)

        with sp.Fori(1, 5) as gp:
            for h in range(2):
                for b in range(GB):
                    load_block(sp, 2 * GB * gp + GB * h + b, b % RING,
                               w_in3[:, KB * b:KB * b + KB, bass.ds(W1ROWS + 1024 * (gp - 1) + 512 * h, 512)])
                    u2 = b - 2 + GB * h
                    if 0 <= u2 < 8:
                        later_ada_load(gp + 3, 2 * u2)
                        later_ada_load(gp + 3, 2 * u2 + 1)

        def pair_load(p):
            for i in range(2):
                load_block(sp, N_MLA + 4 * p + i, i,
                           w_uq3[:, 2 * i:2 * i + 2, bass.ds(2 * QK * p, 2 * QK)], 2 * QK)
            for i in range(2):
                load_block(sp, N_MLA + 4 * p + 2 + i, 2 + i,
                           w_ukv3[:, i:i + 1, bass.ds(512 * p, 512)], 512, 1)

        def pair_store(p):
            for h in range(2):
                sp.wait_ge(a_olo, 2 * p + h + 1)
                sp.dma_start(mix_d[:, bass.ds(2 * p + h, 1), :, :].rearrange("p a b n -> p (a b) n"),
                             ost[:, h, :, :]).then_inc(mix_stored[h], 16)
        pair_load(0)
        pair_load(1)
        sp.wait_ge(g_rows, 1)
        sp.dma_start(g_d, grw).then_inc(g_stored, 16)
        with sp.Fori(0, PAIRS - 2) as p:
            pair_load(p + 2)
            pair_store(p)

        def out_load(g, b):
            load_block(sp, N_OUT + GB * g + b, b % RING,
                       w_out3[:, KB * b:KB * b + KB, bass.ds(512 * g, 512)])
        pair_store(PAIRS - 2)
        for b in range(3):
            out_load(0, b)

        def scores_load(h, first=False):
            if not first:
                sp.wait_ge(m_QK, TT * h)
            for part in range(2):
                sp.dma_start(mq[part][:, :, :].bitcast(F), qk_d[part, :, bass.ds(2 * h, 2), :]
                             ).then_inc(m_qk_in, 16)
                sp.dma_start(mk[part][:, :, :].bitcast(F), qk_d[part, :, bass.ds(8 + 2 * h, 2), :]
                             ).then_inc(m_qk_in, 16)
            if not first:
                sp.wait_ge(m_S, 2 * TT * h)
            sp.dma_start(gb[:, :, :], g_d[bass.ds(h, 1)].rearrange("a d s -> (a d s)")
                         .partition_broadcast(P).rearrange("p (d s) -> p d s", d=2)).then_inc(m_g_in, 16)

        def values_load(h, first=False):
            if not first:
                sp.wait_ge(m_V, 2 * h)
                sp.wait_ge(m_t2, 2 * h)
            for part in range(2):
                sp.dma_start(mv[part][:, :, :].bitcast(F), v_d[part, :, :, bass.ds(DM * h, DM)]
                             ).then_inc(m_v_in, 16)
            sp.dma_start(mo[:, :, :], o_d[:, bass.ds(2 * h, 2), :]).then_inc(m_v_in, 16)
        for s in range(2):
            sp.wait_ge(staged[s], 32 * 12 + 16)
        for b in range(4):
            sp.wait_ge(o_stored[b], 32)
        sp.wait_ge(g_stored, 16)
        sp.wait_ge(blk_done, N_MLA + 4 * PAIRS)
        scores_load(0, True)
        values_load(0, True)
        pair_store(PAIRS - 1)
        scores_load(1)
        for s in range(2):
            sp.wait_ge(mix_stored[s], 16 * PAIRS)
        sp.dma_start(mixA[:, :, :, :].bitcast(F), mix_d[:, 0:NH, :, :]).then_inc(mixA_in, 16)
        with sp.Fori(1, HM - 1) as h:
            scores_load(h + 1)
            values_load(h)
        values_load(HM - 1)

        def out_units(pair, us):
            for u in us:
                later_ada_load(pair, u, araw2)
        for b in range(3, 7):
            out_load(0, b)
        sp.wait_ge(m_olo, 2 * HM)
        sp.wait_ge(xT_stored, 16)
        out_units(8, range(4))
        out_load(0, 7)
        out_units(8, range(4, 8))
        sp.dma_start(x1T[:, :, :], xT_d).then_inc(xT_back, 16)
        with sp.Fori(1, G_OUT) as g:
            for b in range(GB):
                out_load(g, b)
                out_units(7 + g if b < 4 else 8 + g, [(2 * b + 8) % 16, (2 * b + 9) % 16])
        out_units(11, range(8, 16))

        with sp.Fori(0, CHUNKS) as ch:
            for q in range(2):
                for b in range(GB):
                    load_block(sp, N_FF + CB * ch + GB * q + b, b % RING,
                               w_ff13[:, KB * b:KB * b + KB, bass.ds(CH * ch + 512 * q, 512)])
            for q in range(4):
                for b in range(CT // KB):
                    load_block(sp, N_FF + CB * ch + 2 * GB + 4 * q + b, b % RING,
                               w_ff23[:, bass.ds(CT * ch + KB * b, KB), 512 * q:512 * q + 512])

        for t in range(TT):
            sp.wait_ge(y_act, 2 * (t + 1))
            sp.wait_ge(y_dve, 2 * (t + 1))
            sp.dma_start(out[t * P:(t + 1) * P, :], yst[:, t % 2, :]).then_inc(y_stored[t % 2], 16)
        for s in range(2):
            sp.wait_ge(y_stored[s], 16 * TT // 2)

    @block.gpsimd
    def _(pool):
        steps = [0]

        def link(ins):
            steps[0] += 1
            ins.then_inc(pool_step, 1)
        link(pool.memset(ident[:, :], 0.0))
        link(pool.memset(mask[:, :, :], 0.0))
        for i, f in enumerate(rope_freqs()):
            link(pool.memset(freq[:, i:i + 1], float(f)))
        link(pool.memset(ones[:, :], 1.0))
        link(pool.memset(nhalf[:, :], -0.5))
        pool.wait_ge(pool_step, steps[0])
        pool.affine_select(out=ident[:, :], in_=ident[:, :], compare_op=ALU.not_equal, fill=1.0, base=0,
                           pattern=[[-1, P]], channel_multiplier=1).then_inc(const_done, 1)
        pool.affine_select(out=mask[:, 0, :], in_=mask[:, 0, :], compare_op=ALU.is_ge, fill=NEG, base=0,
                           pattern=[[-1, P]], channel_multiplier=1).then_inc(const_done, 1)
        pool.affine_select(out=mask[:, 1, :], in_=mask[:, 1, :], compare_op=ALU.is_ge, fill=NEG, base=0,
                           pattern=[[1, P]], channel_multiplier=-1).then_inc(const_done, 1)

        norm_pow(pool, n1)

        def first_split_lo(n):
            split_lo(pool, n, n % RING, 336 if n < 2 * GB and first_block(n)[0] == 1 else 512)
        for n in range(3):
            first_split_lo(n)
        for q in range(4):
            for k in range(4 * q, 4 * q + 4):
                pool.wait_ge(h_hi, k + 1)
                pool.tensor_tensor(hT[1][:, k, :], utmp[:, k % 2, :], hT[0][:, k, :].bitcast(F),
                                   ALU.subtract).then_inc(h_lo, 1)
            for n in range(4 * q + 3, 4 * q + 7):
                first_split_lo(n)
        for n in range(19, 3 * GB):
            first_split_lo(n)
        pool.wait_ge(low_ms, 1)
        pool.tensor_tensor(rs[:, 0:8], ssq[:, 0:8], nhalf[:, 0:1].to_broadcast([P, 8]),
                           ALU.pow).then_inc(low_rs, 1)
        with pool.Fori(3 * GB // 4, N_MLA // 4) as i:
            for s in range(4):
                split_lo(pool, 4 * i + s, s)
        def pair_split(p):
            for i in range(2):
                split_lo(pool, N_MLA + 4 * p + i, i, 2 * QK)
            for i in range(2):
                split_lo(pool, N_MLA + 4 * p + 2 + i, 2 + i, 512, 1)

        def pair_pow(p):
            for ready, done, o in ((a_qms, a_qrs, 0), (a_kms, a_krs, 8)):
                pool.wait_ge(ready, p + 1)
                pool.tensor_tensor(rs[:, o:o + 8], ssq[:, o:o + 8], nhalf[:, 0:1].to_broadcast([P, 8]),
                                   ALU.pow).then_inc(done, 1)
        pair_split(0)
        pair_pow(0)
        pair_split(1)
        with pool.Fori(0, PAIRS - 2) as p:
            pair_pow(p + 1)
            pair_split(p + 2)
        pair_pow(PAIRS - 1)
        for s in range(3):
            split_lo(pool, N_OUT + s, s)

        def head_mask(h):
            pool.wait_ge(m_g_in, 16 * (h + 1))
            if not (isinstance(h, int) and h == 0):
                pool.wait_ge(m_exp, 14 * h)
            for d in range(2):
                pool.tensor_tensor(gbm[:, d, :].rearrange("p (a n) -> p a n", a=TT),
                                   gb[:, d, :].rearrange("p (a n) -> p a n", a=TT),
                                   mask[:, d, None, :].to_broadcast([P, TT, P]), ALU.add).then_inc(m_mask, 1)
        head_mask(0)
        with pool.Fori(0, HM - 1) as h:
            head_mask(h + 1)
            norm_pow(pool, nm, h)
        norm_pow(pool, nm, HM - 1)
        split_lo(pool, N_OUT + 3, 3)
        with pool.Fori(1, GB * G_OUT // 4) as i:
            for s in range(4):
                split_lo(pool, N_OUT + 4 * i + s, s)
        for s in range(3):
            split_lo(pool, N_FF + s, s)
        norm_pow(pool, n2)
        split_lo(pool, N_FF + 3, 3)
        with pool.Fori(1, CB * CHUNKS // 4) as i:
            for s in range(4):
                split_lo(pool, N_FF + 4 * i + s, s)

    @block.tensor
    def _(pe):
        def passes(dst, lhs, rhs, start, stop):
            pe.matmul(dst, lhs[0], rhs[0], start=start, stop=False)
            pe.matmul(dst, lhs[0], rhs[1], start=False, stop=False)
            return pe.matmul(dst, lhs[1], rhs[0], start=False, stop=stop)

        def wtile(slot, k, lo, hi):
            return [t[:, slot, k, lo:hi] for t in (whi, wlo)]

        def group_block(n, b, half, act_of, blocks, by_tokens, cols=512, kready=None,
                        slot=None, by_quarters=()):
            slot = b % RING if slot is None else slot
            pe.wait_ge(lo_ready, n + 1)
            for k in range(KB):
                kt = KB * b + k
                if kready is not None:
                    kready(kt)
                for m in range(4):
                    first, last = kt == 0, kt == KB * blocks - 1
                    if m in by_quarters:
                        first, last = kt % 4 == 0, kt % 4 == 3
                    if by_tokens:
                        ins = passes(ps[:, 4 * half + m, 0:cols],
                                     [act_of(i, kt)[:, m * P:(m + 1) * P] for i in range(2)],
                                     wtile(slot, k, 0, cols), first, last)
                    else:
                        ins = passes(ps[:, 4 * half + m, :], wtile(slot, k, m * P, (m + 1) * P),
                                     [act_of(i, kt) for i in range(2)], first, last)
            ins.then_inc(blk_done, 1)

        def ada_sum(pair, tile, bank):
            pe.wait_ge(ada_step, 32 * (pair + 1))
            for w in range(2):
                for j in range(4):
                    ins = pe.matmul(ps[:, bank, 4 * w + j:4 * w + j + 1],
                                    tile[:, w, j * P:(j + 1) * P], ones[:, 0:1],
                                    start=True, stop=True)
            ins.then_inc(ada_summed, 1)

        pe.wait_ge(const_done, 3)
        pe.wait_ge(vec_loaded, 16 * 13)
        pe.wait_ge(pos_f, 1)
        pe.transpose(ps[:, 7, 0:V_ROWS], rows0[:, :], ident[0:V_ROWS, 0:V_ROWS])
        pe.transpose(ps[:, 7, V_ADA:V_ADA + 96], rows1[:, :], ident[0:96, 0:96])
        pe.transpose(ps[:, 7, V_CW:V_CW + 80], rows2[:, :], ident[0:80, 0:80])
        pe.transpose(ps[:, 7, V_POS:V_POS + TT], posf[:, :], ident[0:TT, 0:TT]).then_inc(vec_T, 1)
        for t in range(TT):
            pe.wait_ge(x_loaded[t % 2], 16 * (t // 2 + 1))
            if t >= 2:
                pe.wait_ge(x_evac, 4 * (t - 1))
            if t == 1:
                pe.wait_ge(vec_cols, 1)
            for k in range(4):
                for j in range(4):
                    ft = 4 * k + j
                    ins = pe.transpose(ps[:, 4 * (t % 2) + k, j * P:(j + 1) * P],
                                       xnat[:, t % 2, ft * P:(ft + 1) * P], ident[:, :])
                ins.then_inc(x_T, 1)
        pe.wait_ge(x_evac, 4 * TT)
        norm_bcast(pe, n1, 5, utmp[:, 1, :])
        pe.wait_ge(n1[5], 1)

        hin = lambda i, kt: hT[i][:, kt, :]
        for q in range(4):
            if q >= 1:
                pe.wait_ge(ada_read, 2 * q)
                pe.wait_ge(kv_part, q)
            ada_sum(q, acc[:, 2 * (q % 2):2 * (q % 2) + 2, :], 7)
            for n in range(4 * q, 4 * q + 4):
                g, b = first_block(n)
                group_block(n, b, g, hin, GB, True, cols=336 if g == 1 else 512,
                            kready=lambda kt: pe.wait_ge(h_lo, kt + 1), slot=n % RING,
                            by_quarters=(3,) if g == 1 else ())

        def low_transposes(i0, bank):
            pe.wait_ge(low_norm, 8)
            for i in range(3):
                ft = i0 + i
                src = cq[:, :, ft * P:(ft + 1) * P] if ft < 4 else ckv[:, :, (ft - 4) * P:(ft - 3) * P]
                for t in range(TT):
                    ins = pe.transpose(ps[:, bank + i, t * P:(t + 1) * P], src[:, t, :], ident[:, :])
                ins.then_inc(low_T, 1)

        def gate_transposes():
            pe.wait_ge(ada_read, 16)
            for k in range(4):
                for t in range(TT):
                    ins = pe.transpose(ps[0:HM, k, t * P:(t + 1) * P], ckv[:, t, 320 + 4 * k:324 + 4 * k],
                                       ident[:, :])
            ins.then_inc(g_T, 1)

        def in_pair(gp, by_tokens):
            for h in range(2):
                pe.wait_ge(bank_free[h], 4 * gp)
                if h == 0:
                    pe.wait_ge(ada_read, 2 * (gp + 3))
                g = 2 * gp + h
                if isinstance(g, int) and g >= 8:
                    pe.wait_ge(low_lo, 3 * (g - 7))
                for b in range(GB):
                    if b == 5:
                        pe.wait_ge(bank_free[1 - h], 4 * gp + 4 * h)
                        if h == 1:
                            ada_sum(gp + 3, acc[:, 0:2, :], 3)
                        if isinstance(g, int) and g in (7, 8):
                            low_transposes(3 * (g - 7), 4 * (1 - h))
                    if b == 7 and isinstance(g, int) and g == 9:
                        gate_transposes()
                    group_block(GB * (2 * gp + h) + b, b, h, hin, GB, by_tokens)
        with pe.Fori(1, 3) as gp:
            in_pair(gp, False)
        in_pair(3, True)
        in_pair(4, False)

        def project_q(p):
            for i in range(2):
                pe.wait_ge(lo_ready, N_MLA + 4 * p + i + 1)
                for k in range(2):
                    kt = 2 * i + k
                    for t in range(TT):
                        ins = passes(ps[:, 4 + t, 0:2 * QK],
                                     [cqT[j][:, kt, t * P:(t + 1) * P] for j in range(2)],
                                     wtile(i, k, 0, 2 * QK), kt == 0, kt == 3)
                ins.then_inc(blk_done, 1)

        def project_kv(p):
            pe.wait_ge(a_qn, p + 1)
            for i in range(2):
                pe.wait_ge(lo_ready, N_MLA + 4 * p + i + 3)
                for t in range(TT):
                    ins = passes(ps[:, 4 + t, :], [ckvT[j][:, i, t * P:(t + 1) * P] for j in range(2)],
                                 wtile(2 + i, 0, 0, 512), i == 0, i == 1)
                ins.then_inc(blk_done, 1)

        def transpose_qk(p):
            pe.wait_ge(a_qr, p + 1)
            pe.wait_ge(a_kn, p + 1)
            pe.wait_ge(a_vraw, p + 1)
            for h in range(2):
                for t in range(TT):
                    pe.transpose(ps[:, 4 + h, t * P:(t + 1) * P], qn[:, t, h, 0:NOPE], ident[:, :])
            for t in range(TT):
                ins = pe.transpose(ps[:, 6, t * P:(t + 1) * P],
                                   qr[:, t, :, :].rearrange("p h d -> p (h d)"), ident[:, :])
            ins.then_inc(a_Tq, 1)
            for j, bank in enumerate((7, 4, 5)):
                if j == 1:
                    pe.wait_ge(a_qTlo, p + 1)
                for t in range(TT):
                    src = kn[:, t, j, :] if j < 2 else kr[:, t, :, :].rearrange("p h d -> p (h d)")
                    ins = pe.transpose(ps[:, bank, t * P:(t + 1) * P], src, ident[:, :])
                ins.then_inc(a_Tk, 1)

        def scores(p, h):
            if h == 0:
                pe.wait_ge(a_kTlo, 3 * (p + 1))
            for t in range(TT):
                if t == 3 and not (isinstance(p, int) and p == 0 and h == 0):
                    pe.wait_ge(a_olo, 2 * p + h)
                q = slice(t * P, (t + 1) * P)
                r = slice(ROPE * h, ROPE * h + ROPE)
                passes(ps[:, t, :], [qT[i][:, h, q] for i in range(2)],
                       [kT[i][:, h, :] for i in range(2)], True, False)
                passes(ps[:, t, :], [qT[i][r, 2, q] for i in range(2)],
                       [kT[i][r, 2, :] for i in range(2)], False, True).then_inc(a_S, 1)

        def prob_transposes(p, h):
            for t in range(TT):
                pe.wait_ge(a_prob, 8 * p + 4 * h + t + 1)
                for j in range(TT):
                    ins = pe.transpose(ps[:, t, j * P:(j + 1) * P], pr[:, t, j * P:(j + 1) * P], ident[:, :])
                ins.then_inc(a_PT, 1)

        def values(p, h):
            pe.wait_ge(a_PTlo, 8 * p + 4 * h + 4)
            pe.wait_ge(a_vlo, p + 1)
            for j in range(TT):
                ins = passes(ps[:, 3, :], [vv[i][:, j, h, :] for i in range(2)],
                             [pT[i][:, j, :] for i in range(2)], j == 0, j == TT - 1)
            ins.then_inc(a_PV, 1)

        def pair(p, nxt):
            scores(p, 0)
            if nxt:
                project_q(p + 1)
            prob_transposes(p, 0)
            values(p, 0)
            if nxt:
                project_kv(p + 1)
            scores(p, 1)
            prob_transposes(p, 1)
            if nxt:
                transpose_qk(p + 1)
            values(p, 1)

        pe.wait_ge(bank_free[1], 20)
        project_q(0)
        project_kv(0)
        pe.wait_ge(g_bias, 4)
        pe.wait_ge(g_rows, 1)
        pe.wait_ge(g_em, 1)
        for w in range(2):
            for d in range(2):
                for t in range(TT):
                    i = (w * 2 + d) * TT + t
                    ins = pe.transpose(ps[:, 0, HM * i:HM * i + HM],
                                       gT[:, 2 * w + d, t * P:(t + 1) * P], ident[0:HM, 0:HM])
        ins.then_inc(g_colT, 1)
        transpose_qk(0)
        pe.wait_ge(g_cols, 1)
        pair(0, True)
        with pe.Fori(1, PAIRS - 1) as p:
            pair(p, True)
        pair(PAIRS - 1, False)

        def head_scores(h):
            pe.wait_ge(m_qk_in, 64 * (h + 1))
            if not (isinstance(h, int) and h == 0):
                pe.wait_ge(m_S, 2 * TT * h)
            for t in range(TT):
                if isinstance(h, int) and h == 0 and t == TT - 1:
                    pe.wait_ge(a_olo, NH)
                for k in range(2):
                    ins = passes(ps[:, t, :], [mq[i][:, k, t * P:(t + 1) * P] for i in range(2)],
                                 [mk[i][:, k, :] for i in range(2)], k == 0, k == 1)
                ins.then_inc(m_QK, 1)

        def head(h, nxt):
            for i, t in enumerate(WT_ORDER):
                if not (isinstance(h, int) and h == 0):
                    pe.wait_ge(m_normed, 2 * h) if t < 2 else pe.wait_ge(nm[5], h)
                pe.wait_ge(m_w, TT * h + t + 1)
                for j in range(TT):
                    ins = pe.transpose(ps[:, 4 + t, j * P:(j + 1) * P], sf[:, t, j * P:(j + 1) * P],
                                       ident[:, :])
                ins.then_inc(m_WT, 1)
            if nxt:
                head_scores(h + 1)
            else:
                pe.wait_ge(m_S, 2 * TT * HM)
                pe.wait_ge(mixA_in, 16)
                group_block(N_OUT, 0, 0, mix, GB, False)
            pe.wait_ge(m_v_in, 48 * (h + 1))
            pe.wait_ge(m_WTlo, TT * (h + 1))
            for v in range(2):
                for j in range(TT):
                    ins = passes(ps[:, 4 + v, :], [mv[i][:, j, v * P:(v + 1) * P] for i in range(2)],
                                 [wT[i][:, j, :] for i in range(2)], j == 0, j == TT - 1)
                ins.then_inc(m_V, 1)
            if not nxt:
                group_block(N_OUT + 1, 1, 0, mix, GB, False)
            pe.wait_ge(m_sq, 2 * h + 2)
            norm_sum(pe, nm, 6, [msq[:, v, :] for v in range(2)])
            norm_bcast(pe, nm, 7, msq[:, 0, :], h)
            if not nxt:
                group_block(N_OUT + 2, 2, 0, mix, GB, False)
        head_scores(0)
        head(0, True)
        with pe.Fori(1, HM - 1) as h:
            head(h, True)
        head(HM - 1, False)

        def out_pair(gp, start=0):
            for h in range(2):
                g = 2 * gp + h
                if not (h == 0 and start):
                    pe.wait_ge(o_free[h], 4 * gp + 4)
                    pe.wait_ge(ada_read, 2 * (7 + g))
                for b in range(GB):
                    if h == 0 and b < start:
                        continue
                    if b == 4 and not (isinstance(g, int) and g == 0):
                        pe.wait_ge(o_free[1 - h], 4 * gp + 4 + 4 * h)
                        ada_sum(7 + g, acc2[:, 2 * (1 - h):2 * (1 - h) + 2, :], 4 * (1 - h) + 3)
                    group_block(N_OUT + GB * g + b, b, h, mix, GB, False)
        pe.wait_ge(m_olo, 2 * HM)
        out_pair(0, 3)
        with pe.Fori(1, G_OUT // 2) as gp:
            out_pair(gp)
        pe.wait_ge(o_sqadd, KT + 1)
        pe.wait_ge(o_free[0], 12)
        ada_sum(11, acc2[:, 2:4, :], 3)
        norm_sum(pe, n2, 0, [sqacc2[:, :]])
        norm_bcast(pe, n2, 1, utmp2[:, 1, :])
        pe.wait_ge(o_free[1], 12)
        pe.wait_ge(n2[5], 1)
        pe.wait_ge(ada_read, 24)

        with pe.Fori(0, CHUNKS) as ch:
            for q in range(2):
                pe.wait_ge(f_free[q], 12 * ch + 4)
                for b in range(GB):
                    group_block(N_FF + CB * ch + GB * q + b, b, q, lambda i, kt: h2T[i][:, kt, :], GB, False,
                                kready=(lambda kt: pe.wait_ge(h2_lo, kt + 1)) if q == 0 else None)
            for q in range(4):
                pe.wait_ge(f_free[q % 2], 12 * ch + 4 * (q // 2 + 2))
                for b in range(CT // KB):
                    group_block(N_FF + CB * ch + 2 * GB + 4 * q + b, b, q % 2,
                                lambda i, kt: aT[i][:, kt, :], CT // KB, False,
                                kready=(lambda kt: pe.wait_ge(f_lo, CT * ch + kt + 2)) if q == 0 else None)

        pe.wait_ge(f_free[0], 12 * CHUNKS + 4)
        pe.wait_ge(f_free[1], 12 * CHUNKS + 4)
        for t in range(TT):
            if t >= 2:
                pe.wait_ge(y_act, 2 * (t - 1))
                pe.wait_ge(y_dve, 2 * (t - 1))
            for k in range(4):
                for j in range(4):
                    ins = pe.transpose(ps[:, 4 * (t % 2) + k, j * P:(j + 1) * P],
                                       x1T[:, 4 * k + j, t * P:(t + 1) * P], ident[:, :])
                ins.then_inc(y_T, 1)

    @block.scalar
    def _(act):
        for t in range(2):
            act.dma_start(xnat[:, t, :], x[t * P:(t + 1) * P, :]).then_inc(x_loaded[t], 16)
        act.wait_ge(vec_cols, 1)
        act.activation(silc[:, :], VT[:, V_C:V_C + KT], ACT.Silu).then_inc(silc_done, 1)
        for t in range(TT):
            act.wait_ge(x_loaded[t % 2], 16 * (t // 2 + 1))
            act.activation(xsq[:, t, :], xnat[:, t % 2, :], ACT.Square, accum_out=ssq[:, t:t + 1]
                           ).then_inc(n1[0], 1)
            for k in range(4):
                act.wait_ge(x_T, 4 * t + k + 1)
                if t < 2 and k == 3:
                    act.wait_ge(n1[0], t + 1)
                    act.dma_start(xnat[:, t, :], x[(t + 2) * P:(t + 3) * P, :]).then_inc(x_loaded[t], 16)
                act.activation(xT[:, 4 * k:4 * k + 4, t * P:(t + 1) * P],
                               ps[:, 4 * (t % 2) + k, :].rearrange("p (j n) -> p j n", j=4),
                               ACT.Copy).then_inc(x_evac, 1)
        def first_split(n):
            slot, use = n % RING, n // RING + 1
            g, b = first_block(n)
            if g == 0:
                split_hi(act, n, slot, use, first=n < RING)
                return
            act.wait_ge(w_loaded[slot], 16 * use)
            if n >= RING:
                act.wait_ge(blk_done, n - RING + 1)
            act.wait_ge(gate_loaded, 16)
            act.activation(wraw[:, slot, :, 320:336], wgate[:, KB * b:KB * b + KB, :],
                           ACT.Copy).then_inc(act_step, 1)
            act.wait_ge(act_step, 2 * (n // 4) + n % 2 + 1)
            act.activation(whi[:, slot, :, 0:336], wraw[:, slot, :, 0:336], ACT.Copy).then_inc(hi_ready, 1)

        norm_scale(act, n1, 5, rstd[:, :])
        for n in range(3):
            first_split(n)
        act.wait_ge(n1[0], TT)
        for q in range(4):
            for k in range(4 * q, 4 * q + 4):
                act.wait_ge(u_done, k + 1)
                act.activation(utmp[:, k % 2, :], utmp[:, k % 2, :], ACT.Identity,
                               bias=M[:, M_SH1 + k:M_SH1 + k + 1]).then_inc(h_sum, 1)
                act.wait_ge(h_sum, k + 1)
                act.activation(hT[0][:, k, :], utmp[:, k % 2, :], ACT.Copy).then_inc(h_hi, 1)
            if q < 3:
                for n in range(4 * q + 3, 4 * q + 7):
                    first_split(n)
        first_split(2 * GB - 1)
        act.wait_ge(h_lo, KT)
        act.dma_start(xT_d, xT[:, :, :]).then_inc(xT_stored, 16)
        act.wait_ge(blk_done, 2 * GB - 2)
        for t in range(TT):
            act.activation(cq[:, t, :], ps[:, t, :], ACT.Copy).then_inc(bank_free[0], 1)
        for n in range(2 * GB, 2 * GB + 3):
            split_hi(act, n, n % RING, n // RING + 1)
        for b in range(GB):
            n = 2 * GB + b + 3
            split_hi(act, n, n % RING, n // RING + 1)
            if b < TT:
                act.wait_ge(blk_done, 2 * GB)
                if b < TT - 1:
                    act.activation(ckv[:, b, :], ps[:, 4 + b, 0:336], ACT.Copy).then_inc(bank_free[1], 1)
            if b == 4:
                act.wait_ge(bank_free[0], 4)
                act.wait_ge(bank_free[1], 4)
                act.wait_ge(xT_stored, 16)
                junk = sth[:, :, :].rearrange("p a n -> p (a n)")
                for t in range(TT):
                    j = 336 * (t % 2)
                    if t >= 2:
                        act.wait_ge(low_sq, 3 * (t - 1))
                    act.activation(stl[:, t % 2, :], cq[:, t, :], ACT.Square,
                                   accum_out=ssq[:, t:t + 1]).then_inc(low_sq, 1)
                    act.activation(junk[:, j:j + 256], ckv[:, t, 0:256], ACT.Square,
                                   accum_out=ssq[:, 4 + t:5 + t]).then_inc(low_sq, 1)
                    act.activation(junk[:, j + 256:j + 320], ckv[:, t, 256:320], ACT.Square,
                                   accum_out=pess[:, t:t + 1]).then_inc(low_sq, 1)
            if b == 5:
                act.wait_ge(ang_r, 1)
                act.activation(sinT[:, :, :], ang[:, 4, :, :], ACT.Sin).then_inc(trig, 1)
                act.activation(cosT[:, :, :], ang[:, 5, :, :], ACT.Sin).then_inc(trig, 1)

        def store(T, i, qk):
            act.wait_ge(c_lo, T + 2)
            for part, buf in enumerate((sth, stl)):
                if qk:
                    d = qk_d[part, :, bass.ds(T, 1), :].rearrange("p a n -> p (a n)")
                else:
                    d = v_d[part, :, i, 512 * ((T - 16) // 4):512 * ((T - 16) // 4) + 512]
                act.dma_start(d, buf[:, i % 2, :]).then_inc(staged[i % 2], 16)

        def conv_group(g, half, gp):
            T0 = 4 * (g - 3)
            for b in range(GB):
                n = GB * g + b + 3
                split_hi(act, n, (b + 3) % RING, 2 * g + (b + 3) // RING + 1)
                if b < 4:
                    act.wait_ge(blk_done, GB * g)
                    act.wait_ge(c_lo, T0 + max(b - 1, 0) + 1)
                    act.activation(yc[:, b % 2, :], ps[:, 4 * half + b, :], ACT.Identity,
                                   scale=col(VT, V_CW + 32 + T0 + b), bias=col(VT, V_CB + T0 + b)
                                   ).then_inc(c_mid, 1)
                if 1 <= b <= 4:
                    i = b - 1
                    act.wait_ge(bank_free[half], 4 * gp + i + 1)
                    act.activation(yc[:, i % 2, :], yc[:, i % 2, :], ACT.Silu).then_inc(c_silu, 1)
                    act.wait_ge(c_silu, T0 + i + 1)
                    act.wait_ge(staged[i % 2], 16 * (T0 + 2 * (i // 2) + 1))
                    act.activation(sth[:, i % 2, :].bitcast(R), yc[:, i % 2, :], ACT.Copy).then_inc(c_hi, 1)
                if 2 <= b <= 5:
                    store(T0 + b - 2, (b - 2) % 4, True)

        act.wait_ge(low_sq, 12)
        for i in range(2):
            act.sem_inc(staged[i], 16)
        with act.Fori(1, 3) as gp:
            conv_group(2 * gp + 1, 0, gp)
            conv_group(2 * gp + 2, 1, gp)

        def v_group(g, half):
            T0 = 4 * (g - 3)
            for b in range(GB):
                n = GB * g + b + 3
                split_hi(act, n, (b + 3) % RING, 2 * g + (b + 3) // RING + 1)
                if b < 4:
                    act.wait_ge(blk_done, GB * g)
                    act.wait_ge(staged[b % 2], 16 * (T0 + 2 * (b // 2) + 1))
                    act.activation(sth[:, b % 2, :].bitcast(R), ps[:, 4 * half + b, :], ACT.Copy
                                   ).then_inc(c_hi, 1)
                if 1 <= b <= 4:
                    store(T0 + b - 1, b - 1, False)
                if b == 6:
                    for i in range(3):
                        ft = 3 * (g - 7) + i
                        act.wait_ge(low_T, ft + 1)
                        act.activation(cqT[0][:, ft, :] if ft < 4 else ckvT[0][:, ft - 4, :],
                                       ps[:, 4 * half + i, :], ACT.Copy,
                                       scale=VT[:, V_QG + ft:V_QG + ft + 1]).then_inc(low_hi, 1)

        def o_group(g, half):
            for b in range(GB):
                n = GB * g + b + 3
                if n < N_MLA:
                    split_hi(act, n, (b + 3) % RING, 2 * g + (b + 3) // RING + 1)
                if b < 4:
                    i = 4 * (g - 9) + b
                    act.wait_ge(blk_done, GB * g)
                    if g == 9:
                        act.wait_ge(staged[b % 2], 32 * 12 + 16)
                    else:
                        act.wait_ge(o_stored[b], 16)
                    buf = (sth, stl)[b // 2]
                    act.activation(buf[:, b % 2, :], ps[:, 4 * half + b, :], ACT.Sigmoid
                                   ).then_inc(bank_free[half], 1)
                    act.wait_ge(bank_free[half], 16 + b + 1)
                    act.dma_start(o_d[:, i, :], buf[:, b % 2, :]).then_inc(o_stored[b], 16)
        v_group(7, 0)
        v_group(8, 1)
        o_group(9, 0)
        def mla_split(p, i):
            n = N_MLA + 4 * p + i
            split_hi(act, n, i, N_MLA // RING + p + 1, 2 * QK if i < 2 else 512, 2 if i < 2 else 1)
        for i in range(3):
            mla_split(0, i)
        o_group(10, 1)
        mla_split(0, 3)

        for d in range(2):
            act.wait_ge(g_bias, 4 + d + 1)
            act.activation(gw[:, d, :], gw[:, d, :], ACT.Exp, scale=-1.0).then_inc(g_exp, 1)
        for d in range(2):
            act.wait_ge(g_exp, d + 1)
            act.activation(gw[:, d, :], gw[:, d, :], ACT.Ln, bias=1.0).then_inc(g_ln, 1)

        def q_squares(p):
            act.wait_ge(blk_done, N_MLA + 4 * p + 2)
            act.activation(qn[:, :, :, :].rearrange("p t h d -> p t (h d)"), ps[:, 4:8, 0:2 * QK],
                           ACT.Square).then_inc(a_qsq, 1)

        def kv_out(p):
            act.wait_ge(blk_done, N_MLA + 4 * p + 4)
            kv = ps[:, 4:8, :].rearrange("p t (h e) -> p t h e", h=2)
            act.activation(kn[:, :, :, :], kv[:, :, :, 0:NOPE], ACT.Square).then_inc(a_ksq, 1)
            if not (isinstance(p, int) and p == 0):
                act.wait_ge(a_vlo, p)
            act.activation(vraw[:, :, :, :], kv[:, :, :, NOPE:], ACT.Copy).then_inc(a_vraw, 1)

        def qk_hi(p):
            act.wait_ge(a_Tq, p + 1)
            act.activation(qT[0][:, :, :], ps[:, 4:7, :], ACT.Copy).then_inc(a_qThi, 1)
            for j, bank in enumerate((7, 4, 5)):
                act.wait_ge(a_Tk, 3 * p + j + 1)
                act.activation(kT[0][:, j, :], ps[:, bank, :], ACT.Copy).then_inc(a_kThi, 1)

        def v_hi(p):
            act.wait_ge(a_vraw, p + 1)
            act.activation(vv[0][:, :, :, :], vraw[:, :, :, :], ACT.Copy).then_inc(a_vhi, 1)

        def softmax_exp(p, h, t):
            i = 4 * h + t
            act.wait_ge(a_max, 8 * p + i + 1)
            if t == 0 and not (isinstance(p, int) and p == 0 and h == 0):
                act.wait_ge(a_PT, 8 * p + 4 * h)
            act.activation(pr[:, t, :], ps[:, t, :], ACT.Exp, scale=float(QK) ** -0.5,
                           bias=nms[:, i:i + 1], accum_out=den[:, i:i + 1]).then_inc(a_exp, 1)

        def probT_hi(p, h, t):
            act.wait_ge(a_PT, 8 * p + 4 * h + t + 1)
            if t == 0 and not (isinstance(p, int) and p == 0 and h == 0):
                act.wait_ge(a_PV, 2 * p + h)
            act.activation(pT[0][:, :, t * P:(t + 1) * P],
                           ps[:, t, :].rearrange("p (j n) -> p j n", j=TT), ACT.Copy).then_inc(a_PThi, 1)

        def out_hi(p, h):
            act.wait_ge(a_PV, 2 * p + h + 1)
            if not (isinstance(p, int) and p == 0):
                act.wait_ge(mix_stored[h], 16 * p)
            act.activation(ost[:, h, 0, :].bitcast(R), ps[:, 3, :], ACT.Copy).then_inc(a_ohi, 1)

        def pair(p, nxt, splits):
            for t in range(TT):
                softmax_exp(p, 0, t)
            if nxt:
                q_squares(p + 1)
            for t in range(TT):
                probT_hi(p, 0, t)
            out_hi(p, 0)
            if nxt:
                kv_out(p + 1)
            splits()
            for t in range(TT):
                softmax_exp(p, 1, t)
            for t in range(TT):
                probT_hi(p, 1, t)
            if nxt:
                qk_hi(p + 1)
            out_hi(p, 1)
            if nxt:
                v_hi(p + 1)

        def next_splits(p):
            for i in range(4):
                mla_split(p, i)

        def out_splits():
            for i in range(3):
                split_hi(act, N_OUT + i, i, N_OUT // RING + 1)
        for b in range(4):
            act.wait_ge(o_stored[b], 32)
        q_squares(0)
        kv_out(0)
        act.wait_ge(g_rows, 1)
        act.activation(gT[:, 2:4, :], gw[:, 2:4, :], ACT.Exp, scale=-1.0).then_inc(g_em, 1)
        next_splits(1)
        qk_hi(0)
        v_hi(0)
        act.wait_ge(g_stored, 16)
        pair(0, True, lambda: next_splits(2))
        with act.Fori(1, PAIRS - 2) as p:
            pair(p, True, lambda: next_splits(p + 2))
        pair(PAIRS - 2, True, lambda: None)
        pair(PAIRS - 1, False, out_splits)

        def head_exp(h):
            act.wait_ge(m_mask, 2 * (h + 1))
            for t in range(TT):
                if t >= 2:
                    act.wait_ge(m_S, 2 * TT * h + 2 * (t - 1))
                elif not (isinstance(h, int) and h == 0):
                    act.wait_ge(m_S, 2 * TT * h)
                wf = (t + 1) * P
                dg = slice(t * P, wf)
                for d, (off, to_off, to_dg) in enumerate((
                        (slice(0, t * P), slice(0, t * P), dg),
                        (slice(wf, S), slice(wf + P, wf + S - t * P), slice(wf, wf + P)))):
                    bias = gcol[:, 0, d, t, bass.ds(h, 1)]
                    if off.stop > off.start:
                        act.activation(et[:, t % 2, to_off], gb[:, d, off], ACT.Exp, bias=bias
                                       ).then_inc(m_exp, 1)
                    act.activation(et[:, t % 2, to_dg], gbm[:, d, dg], ACT.Exp, bias=bias).then_inc(m_exp, 1)

        def head_scale(h):
            act.wait_ge(m_rd, h + 1)
            for t in range(TT):
                wf = (t + 1) * P
                act.activation(sf[:, t, 0:wf], sf[:, t, 0:wf], ACT.Copy, scale=mrd[:, 0, t:t + 1]
                               ).then_inc(m_sc, 1)
                if wf < S:
                    act.activation(sf[:, t, wf:S], sbw[:, t, wf:S], ACT.Copy, scale=mrd[:, 1, t:t + 1]
                                   ).then_inc(m_sc, 1)

        def head(h, nxt):
            for i, t in enumerate(WT_ORDER):
                act.wait_ge(m_WT, TT * h + i + 1)
                act.activation(wT[0][:, :, t * P:(t + 1) * P],
                               ps[:, 4 + t, :].rearrange("p (j n) -> p j n", j=TT), ACT.Copy
                               ).then_inc(m_WThi, 1)
            if nxt:
                head_exp(h + 1)
            for v in range(2):
                act.wait_ge(m_V, 2 * h + v + 1)
                act.activation(msq[:, v, :], ps[:, 4 + v, :], ACT.Square).then_inc(m_sq, 1)
            if nxt:
                head_scale(h + 1)
            norm_scale(act, nm, 7, msq[:, 1, :], h)
            for v in range(2):
                act.wait_ge(m_t2, 2 * h + v + 1)
                act.activation(mixM[:, bass.ds(2 * h + v, 1), 0, :].rearrange("p a n -> p (a n)"),
                               mt[:, v, :], ACT.Copy).then_inc(m_ohi, 1)
        act.wait_ge(g_cols, 1)
        head_exp(0)
        head_scale(0)
        for s in range(2):
            act.wait_ge(mix_stored[s], 16 * PAIRS)
        with act.Fori(0, HM - 1) as h:
            head(h, True)
        head(HM - 1, False)

        def out_step(g, b):
            n = N_OUT + GB * g + b + 3
            split_hi(act, n, (b + 3) % RING, N_OUT // RING + 2 * g + (b + 3) // RING + 1)

        for b in range(GB):
            out_step(0, b)
        with act.Fori(1, G_OUT) as g:
            for b in range(GB):
                if b == 0:
                    for i in range(4):
                        T = 4 * (g - 1) + i
                        act.wait_ge(x1_done, T + 1)
                        act.wait_ge(o_sqadd, T if i >= 2 else 4 * (g - 1) + 1)
                        act.activation(sq2[:, i % 2, :], one(x1T, T), ACT.Square).then_inc(o_sq, 1)
                out_step(g, b)
        for i in range(4):
            T = 4 * (G_OUT - 1) + i
            act.wait_ge(x1_done, T + 1)
            act.wait_ge(o_sqadd, T)
            act.activation(sq2[:, i % 2, :], x1T[:, T, :], ACT.Square).then_inc(o_sq, 1)
        norm_scale(act, n2, 1, rstd2[:, :])

        def ff_split(ch, s):
            split_hi(act, N_FF + CB * ch + s + 3, (s + 3) % RING,
                     N_FF // RING + CB // RING * ch + (s + 3) // RING + 1)
        for k in range(KT):
            act.wait_ge(u2_done, k + 1)
            act.activation(h2T[0][:, k, :], utmp2[:, k % 2, :], ACT.Identity,
                           bias=M[:, M_SH2 + k:M_SH2 + k + 1]).then_inc(h2_hi, 1)
            if k in (5, 9, 13):
                ff_split(0, (k - 5) // 4)

        def ff_chunk(ch, first=False, last=False):
            for s in range(CB):
                if not (first and s < 3) and not (last and s + 3 >= CB):
                    ff_split(ch, s)
                if s in (GB, 2 * GB):
                    q = s // GB - 1
                    act.wait_ge(blk_done, N_FF + CB * ch + s)
                    T0 = CT * ch + 4 * q
                    for i in range(5):
                        if i < 4:
                            act.wait_ge(f_sq, T0 + max(i - 1, 0) + 1)
                            act.activation(utmp2[:, i % 2, :], ps[:, 4 * q + i, :], ACT.Relu
                                           ).then_inc(f_relu, 1)
                        if i >= 1:
                            act.wait_ge(f_sq, T0 + i + 1)
                            act.activation(aT[0][:, 4 * q + i - 1, :], sq2[:, (i - 1) % 2, :], ACT.Copy
                                           ).then_inc(f_hi, 1)
        ff_chunk(0, first=True)
        with act.Fori(1, CHUNKS - 1) as ch:
            ff_chunk(ch)
        ff_chunk(CHUNKS - 1, last=True)
        for t in range(TT):
            if t >= 2:
                act.wait_ge(y_stored[t % 2], 16)
            for k in range(0, 4, 2):
                act.wait_ge(y_T, 4 * t + k + 1)
                act.activation(yst[:, t % 2, 512 * k:512 * k + 512], ps[:, 4 * (t % 2) + k, :], ACT.Copy
                               ).then_inc(y_act, 1)

    @block.vector
    def _(dve):
        chain = [0, 0]

        def link(ins):
            chain[0] += 1
            ins.then_inc(dve_step, 1)

        def sync():
            dve.wait_ge(dve_step, chain[0] + chain[1])

        def looped(start, end, per, body):
            before = chain[0]
            with dve.Fori(start, end) as i:
                chain[1] = per * (i - start) if start else per * i
                body(i)
            assert chain[0] - before == per, chain[0] - before
            chain[0], chain[1] = before + per * (end - start), 0

        dve.wait_ge(vec_loaded, 16 * 13)
        dve.tensor_copy(posf[:, :], posi[:, :]).then_inc(pos_f, 1)
        dve.wait_ge(vec_T, 1)
        dve.tensor_copy(VT[:, :], ps[:, 7, 0:V_ALL]).then_inc(vec_cols, 1)
        dve.wait_ge(vec_cols, 1)
        dve.wait_ge(silc_done, 1)

        def ada_units(pair, us, raw=araw, tile=acc[:, 0:2, :], same=True):
            for u2 in us:
                for kk in range(2):
                    for w in range(2):
                        i = 4 * u2 + 2 * kk + w
                        kt = 2 * u2 + kk
                        unit = 2 * u2 + w
                        if kk == 0:
                            dve.wait_ge(ada_loaded[unit % 4], 16 * (4 * pair + unit // 4 + 1))
                        src = raw[:, unit % 4, kk, :]
                        dst = tile[:, w, :]
                        if kt == 0:
                            if same:
                                dve.wait_ge(ada_summed, pair)
                            elif not isinstance(pair, int) or pair >= 2:
                                dve.wait_ge(ada_summed, pair - 1)
                            dve.tensor_scalar(dst, src, silc[:, kt:kt + 1], None, ALU.mult).then_inc(ada_step, 1)
                        else:
                            dve.wait_ge(ada_step, 32 * pair + i - 1)
                            dve.scalar_tensor_tensor(dst, src, silc[:, kt:kt + 1], dst, ALU.mult, ALU.add
                                                     ).then_inc(ada_step, 1)

        def ada_cols(pair, bank, m0, m1, at=0):
            dve.wait_ge(ada_summed, pair + 1)
            for w, m in enumerate((m0, m1)):
                dve.tensor_tensor(M[:, bass.ds(m, 4)], ps[:, bank, at + 4 * w:at + 4 * w + 4],
                                  VT[:, bass.ds(V_ADA + m, 4)], ALU.add).then_inc(ada_read, 1)

        def modulate(ks, src, gain, rst, tmp, s_u, s_lo, rest=None, beside=lambda i: None):
            for k in list(ks) + [None]:
                if k is not None:
                    if k >= 2:
                        dve.wait_ge(s_lo, k - 1)
                    dve.scalar_tensor_tensor(tmp[:, k % 2, :], src[:, k, :], gain[:, k:k + 1], rst[:, :],
                                             ALU.mult, ALU.mult).then_inc(s_u, 1)
                j = ks[-1] if k is None else k - 1
                if rest is not None and j >= ks[0]:
                    rest(j)
                if k is not None:
                    beside(k - ks[0])

        def kv_quarter(q):
            dve.wait_ge(blk_done, 4 * q + 4)
            if q == 0:
                return dve.tensor_copy(ckv[:, 3, :], ps[:, 7, 0:336])
            dve.wait_ge(kv_part, q)
            return dve.tensor_tensor(ckv[:, 3, :], ckv[:, 3, :], ps[:, 7, 0:336], ALU.add)

        def quarter_units(q, us):
            ada_units(q, us, tile=acc[:, 2 * (q % 2):2 * (q % 2) + 2, :], same=False)
        quarter_units(0, range(6))
        dve.wait_ge(n1[0], TT)
        dve.tensor_scalar(rc[:, 0, :], ssq[:, 0:TT], 1.0 / D, EPS, ALU.mult, ALU.add).then_inc(n1[1], 1)
        quarter_units(0, range(6, 7))
        norm_diag(dve, n1, utmp[:, 1, :])
        quarter_units(0, range(7, 8))
        for q in range(4):
            if q >= 1:
                quarter_units(q, range(4, 7))
                kv_quarter(q - 1).then_inc(kv_part, 1)
                quarter_units(q, range(7, 8))
            ada_cols(q, 7, M_SH1 + 4 * q, M_SC1 + 4 * q)
            dve.wait_ge(ada_read, 2 * (q + 1))
            link(dve.scalar_tensor_tensor(A1[:, 4 * q:4 * q + 4], M[:, M_SC1 + 4 * q:M_SC1 + 4 * q + 4], 1.0,
                                          VT[:, V_GMIX + 4 * q:V_GMIX + 4 * q + 4], ALU.add, ALU.mult))
            sync()
            if q == 0:
                dve.wait_ge(n1[5], 1)
                dve.wait_ge(x_evac, 4 * TT)
            modulate(range(4 * q, 4 * q + 4), xT, A1, rstd, utmp, u_done, h_lo,
                     beside=lambda i: quarter_units(q + 1, [i]) if q < 3 else None)
        kv_quarter(3).then_inc(bank_free[1], 1)
        ada_units(4, range(2))

        def step(ins):
            link(ins)
            sync()

        def angles():
            dve.wait_ge(xT_stored, 16)
            link(dve.tensor_tensor(ang[:, 0, :, :], VT[:, V_POS:V_POS + TT, None].to_broadcast([P, TT, ROPE // 2]),
                                   freq[:, None, :].to_broadcast([P, TT, ROPE // 2]), ALU.mult))
            sync()
            big = 12582912.0
            two_pi = 2 * np.pi
            c1 = 6.28125
            c2 = float(np.float32(np.round((two_pi - c1) * 2 ** 20) / 2 ** 20))
            c3 = float(two_pi - c1 - c2)

            a = lambda i: ang[:, i, :, :]
            step(dve.tensor_scalar(a(1), a(0), float(1 / two_pi), big, ALU.mult, ALU.add))
            step(dve.tensor_scalar(a(1), a(1), big, None, ALU.subtract))
            step(dve.tensor_scalar(a(2), a(1), 1.0 / 2048, big, ALU.mult, ALU.add))
            step(dve.tensor_scalar(a(2), a(2), big, 2048.0, ALU.subtract, ALU.mult))
            step(dve.tensor_tensor(a(3), a(1), a(2), ALU.subtract))
            for cc in (c1, c2):
                for kk in (2, 3):
                    step(dve.scalar_tensor_tensor(a(0), a(kk), -cc, a(0), ALU.mult, ALU.add))
            step(dve.scalar_tensor_tensor(a(0), a(1), -c3, a(0), ALU.mult, ALU.add))
            pi = float(np.float32(3.1415925))
            step(dve.tensor_scalar(a(4), a(0), pi, -pi, ALU.min, ALU.max))
            step(dve.tensor_scalar(a(1), a(0), float(np.pi / 2), None, ALU.add))
            step(dve.tensor_scalar(a(2), a(1), pi, -float(two_pi), ALU.is_gt, ALU.mult))
            step(dve.tensor_tensor(a(1), a(1), a(2), ALU.add))
            dve.tensor_scalar(a(5), a(1), pi, -pi, ALU.min, ALU.max).then_inc(ang_r, 1)

        def in_steps(pair, even, piece):
            for b in range(GB):
                piece(b)
                if even and b < 6:
                    ada_units(pair, [b + 2])
                elif not even and b >= 6:
                    if b == 6:
                        m = M_G1 + 8 * (pair - 4)
                        ada_cols(pair, 3, m, m + 4)
                    if ada_on[0]:
                        ada_units(pair + 1, [b - 6])
        ada_on = [True]

        def low_piece(b):
            if b == 4:
                angles()
            if b == 6:
                dve.wait_ge(low_sq, 12)
                link(dve.tensor_scalar(ssq[:, 0:4], ssq[:, 0:4], 1.0 / QL, EPS, ALU.mult, ALU.add))
                dve.tensor_scalar(ssq[:, 4:8], ssq[:, 4:8], 1.0 / KVL, EPS, ALU.mult, ALU.add
                                  ).then_inc(low_ms, 1)
                link(dve.tensor_tensor(ckv[:, :, 256:320], ckv[:, :, 256:320],
                                       kg[:, None, NOPE:QK].to_broadcast([P, TT, ROPE]), ALU.mult))
                sync()
                dve.wait_ge(trig, 2)
                x1, x2 = ckv[:, :, 256:288], ckv[:, :, 288:320]
                tmp = [ang[:, i, :, :] for i in range(4)]
                link(dve.tensor_tensor(tmp[0], x1, cosT[:, :, :], ALU.mult))
                link(dve.tensor_tensor(tmp[1], x2, sinT[:, :, :], ALU.mult))
                link(dve.tensor_tensor(tmp[2], x1, sinT[:, :, :], ALU.mult))
                link(dve.tensor_tensor(tmp[3], x2, cosT[:, :, :], ALU.mult))
                sync()
                link(dve.tensor_tensor(rp[:, :, 0:32], tmp[0], tmp[1], ALU.subtract))
                link(dve.tensor_tensor(rp[:, :, 32:64], tmp[2], tmp[3], ALU.add))
            if b == 7:
                dve.wait_ge(low_rs, 1)
                for t in range(TT):
                    dve.tensor_scalar(cq[:, t, :], cq[:, t, :], rs[:, t:t + 1], None, ALU.mult
                                      ).then_inc(low_norm, 1)
                    dve.tensor_scalar(ckv[:, t, 0:256], ckv[:, t, 0:256], rs[:, 4 + t:5 + t], None, ALU.mult
                                      ).then_inc(low_norm, 1)

        in_steps(4, True, low_piece)

        def conv_piece(g, half, gp):
            T0 = 4 * (g - 3)

            def piece(b):
                if b < 4:
                    y, p = yc[:, b % 2, :], ps[:, 4 * half + b, :]
                    dve.wait_ge(c_mid, T0 + b + 1)
                    for j, (tap, dst, src) in enumerate((
                            (0, slice(2, S), slice(0, S - 2)), (1, slice(1, S), slice(0, S - 1)),
                            (3, slice(0, S - 1), slice(1, S)), (4, slice(0, S - 2), slice(2, S)))):
                        ins = dve.scalar_tensor_tensor(y[:, dst], p[:, src], col(VT, V_CW + 16 * tap + T0 + b),
                                                       y[:, dst], ALU.mult, ALU.add)
                        if j < 3:
                            ins.then_inc(tap_step, 1)
                            dve.wait_ge(tap_step, 3 * (T0 + b) + j + 1)
                        else:
                            ins.then_inc(bank_free[half], 1)
                if 1 <= b <= 4:
                    i = b - 1
                    dve.wait_ge(c_hi, T0 + i + 1)
                    dve.tensor_tensor(stl[:, i % 2, :].bitcast(R), yc[:, i % 2, :], sth[:, i % 2, :],
                                      ALU.subtract).then_inc(c_lo, 1)
            return piece
        dve.sem_inc(c_lo, 1)
        with dve.Fori(1, 3) as gp:
            in_steps(gp + 3, False, conv_piece(2 * gp + 1, 0, gp))
            in_steps(gp + 4, True, conv_piece(2 * gp + 2, 1, gp))

        def v_piece(g, half):
            T0 = 4 * (g - 3)

            def piece(b):
                if b < 4:
                    dve.wait_ge(c_hi, T0 + b + 1)
                    dve.tensor_tensor(stl[:, b % 2, :].bitcast(R), ps[:, 4 * half + b, :], sth[:, b % 2, :],
                                      ALU.subtract).then_inc(c_lo, 1)
                if b == 4:
                    dve.wait_ge(c_lo, T0 + 5)
                    dve.sem_inc(bank_free[half], 4)
                if b == 7:
                    for i in range(3):
                        ft = 3 * (g - 7) + i
                        dst, hi = ((cqT[1][:, ft, :], cqT[0][:, ft, :]) if ft < 4
                                   else (ckvT[1][:, ft - 4, :], ckvT[0][:, ft - 4, :]))
                        dve.wait_ge(low_hi, ft + 1)
                        dve.scalar_tensor_tensor(dst, ps[:, 4 * half + i, :], VT[:, V_QG + ft:V_QG + ft + 1],
                                                 hi.bitcast(F), ALU.mult, ALU.subtract).then_inc(low_lo, 1)
            return piece
        in_steps(6, False, v_piece(7, 0))
        in_steps(7, True, v_piece(8, 1))
        ada_on[0] = False
        in_steps(7, False, lambda b: None)

        dve.wait_ge(g_T, 1)
        for k in range(4):
            dve.tensor_scalar(gT[:, k, :], ps[0:HM, k, :], bgate[:, k:k + 1], None, ALU.add
                              ).then_inc(g_bias, 1)
        dve.wait_ge(g_bias, 4)
        for d in range(2):
            f = gT[:, 2 * d + 1, :]
            dve.scalar_tensor_tensor(gw[:, d, :], f, -1.0, f, ALU.mult, ALU.max).then_inc(g_bias, 1)

        def mean_q(p):
            dve.wait_ge(a_qsq, p + 1)
            link(dve.reduce_sum(ssq[:, 0:8], qn[:, :, :, :].rearrange("p t h d -> p (t h) d"), AX.X))
            sync()
            dve.tensor_scalar(ssq[:, 0:8], ssq[:, 0:8], 1.0 / QK, EPS, ALU.mult, ALU.add).then_inc(a_qms, 1)

        def norm_q(p):
            dve.wait_ge(a_qrs, p + 1)
            for i in range(8):
                t, h = i // 2, i % 2
                ins = dve.scalar_tensor_tensor(qn[:, t, h, :], ps[:, 4 + t, h * QK:(h + 1) * QK],
                                               rs[:, i:i + 1], qg[:, :], ALU.mult, ALU.mult)
            ins.then_inc(a_qn, 1)
            dve.wait_ge(a_qn, p + 1)
            x1, x2 = qn[:, :, :, NOPE:NOPE + 32], qn[:, :, :, NOPE + 32:QK]
            cb = cosT[:, :, None, :].to_broadcast([P, TT, 2, 32])
            sn = sinT[:, :, None, :].to_broadcast([P, TT, 2, 32])
            for i, (a_, b_) in enumerate(((x1, cb), (x2, sn), (x1, sn), (x2, cb))):
                link(dve.tensor_tensor(rt[:, i], a_, b_, ALU.mult))
            sync()
            dve.tensor_tensor(qr[:, :, :, 0:32], rt[:, 0], rt[:, 1], ALU.subtract)
            dve.tensor_tensor(qr[:, :, :, 32:64], rt[:, 2], rt[:, 3], ALU.add).then_inc(a_qr, 1)

        def mean_k(p):
            dve.wait_ge(a_ksq, p + 1)
            link(dve.reduce_sum(ssq[:, 8:16], kn[:, :, :, :].rearrange("p t h d -> p (t h) d"), AX.X))
            sync()
            by_th = ssq[:, 8:16].rearrange("p (t h) -> p t h", h=2)
            link(dve.tensor_tensor(by_th, by_th, pess[:, :, None].to_broadcast([P, TT, 2]), ALU.add))
            sync()
            dve.tensor_scalar(ssq[:, 8:16], ssq[:, 8:16], 1.0 / QK, EPS, ALU.mult, ALU.add).then_inc(a_kms, 1)

        def norm_k(p):
            dve.wait_ge(a_krs, p + 1)
            dve.wait_ge(a_vraw, p + 1)
            for i in range(8):
                t, h = i // 2, i % 2
                dve.scalar_tensor_tensor(kn[:, t, h, :], ps[:, 4 + t, h * 256:h * 256 + NOPE],
                                         rs[:, 8 + i:9 + i], kg[:, 0:NOPE], ALU.mult, ALU.mult)
            dve.tensor_tensor(kr[:, :, :, :], rp[:, :, None, :].to_broadcast([P, TT, 2, ROPE]),
                              rs[:, 8:16].rearrange("p (t h) -> p t h", h=2)[:, :, :, None]
                              .to_broadcast([P, TT, 2, ROPE]), ALU.mult).then_inc(a_kn, 1)

        def qk_lo(p):
            dve.wait_ge(a_qThi, p + 1)
            dve.tensor_tensor(qT[1][:, :, :], ps[:, 4:7, :], qT[0][:, :, :].bitcast(F), ALU.subtract
                              ).then_inc(a_qTlo, 1)
            for j, bank in enumerate((7, 4, 5)):
                dve.wait_ge(a_kThi, 3 * p + j + 1)
                dve.tensor_tensor(kT[1][:, j, :], ps[:, bank, :], kT[0][:, j, :].bitcast(F), ALU.subtract
                                  ).then_inc(a_kTlo, 1)

        def v_lo(p):
            dve.wait_ge(a_vhi, p + 1)
            dve.tensor_tensor(vv[1][:, :, :, :], vraw[:, :, :, :], vv[0][:, :, :, :].bitcast(F), ALU.subtract
                              ).then_inc(a_vlo, 1)

        def softmax(p, h):
            for t in range(TT + 2):
                if t < TT:
                    i = 4 * h + t
                    dve.wait_ge(a_S, 8 * p + i + 1)
                    link(dve.reduce_max(nmax[:, i:i + 1], ps[:, t, :], AX.X))
                    sync()
                    dve.tensor_scalar(nms[:, i:i + 1], nmax[:, i:i + 1], -float(QK) ** -0.5, None, ALU.mult
                                      ).then_inc(a_max, 1)
                if t >= 2:
                    i = 4 * h + t - 2
                    dve.wait_ge(a_exp, 8 * p + i + 1)
                    link(dve.reciprocal(rden[:, i:i + 1], den[:, i:i + 1]))
                    sync()
                    dve.tensor_scalar(pr[:, t - 2, :], pr[:, t - 2, :], rden[:, i:i + 1], None,
                                      ALU.mult).then_inc(a_prob, 1)

        def probT_lo(p, h):
            for t in range(TT):
                dve.wait_ge(a_PThi, 8 * p + 4 * h + t + 1)
                q = slice(t * P, (t + 1) * P)
                dve.tensor_tensor(pT[1][:, :, q], ps[:, t, :].rearrange("p (j n) -> p j n", j=TT),
                                  pT[0][:, :, q].bitcast(F), ALU.subtract).then_inc(a_PTlo, 1)

        def out_lo(p, h):
            dve.wait_ge(a_ohi, 2 * p + h + 1)
            dve.tensor_tensor(ost[:, h, 1, :].bitcast(R), ps[:, 3, :], ost[:, h, 0, :], ALU.subtract
                              ).then_inc(a_olo, 1)

        def pair(p, nxt):
            softmax(p, 0)
            if nxt:
                mean_q(p + 1)
            probT_lo(p, 0)
            if nxt:
                norm_q(p + 1)
            out_lo(p, 0)
            if nxt:
                mean_k(p + 1)
            softmax(p, 1)
            if nxt:
                norm_k(p + 1)
            probT_lo(p, 1)
            if nxt:
                qk_lo(p + 1)
            out_lo(p, 1)
            if nxt:
                v_lo(p + 1)
        mean_q(0)
        norm_q(0)
        dve.wait_ge(g_ln, 2)
        fwd, bwd = slice(None), slice(None, None, -1)
        for d in range(2):
            f = gT[:, 2 * d + 1, :]
            link(dve.scalar_tensor_tensor(gw[:, d, :], f, 0.0, gw[:, d, :], ALU.min, ALU.subtract))
        sync()
        for d, way in enumerate((fwd, bwd)):
            link(dve.tensor_tensor_scan(gw[:, 2 + d, way], gw[:, d, way], gw[:, d, way], 0.0,
                                        ALU.add, ALU.bypass))
        sync()
        for d in range(2):
            link(dve.tensor_tensor(grw[:, d, :], gT[:, 2 * d, :], gw[:, 2 + d, :], ALU.subtract))
        sync()
        for d, way in enumerate((fwd, bwd)):
            link(dve.tensor_tensor_scan(gw[:, d, way], grw[:, d, way], grw[:, d, way], -3.0e38,
                                        ALU.max, ALU.bypass))
        sync()
        link(dve.tensor_tensor(gw[:, 2:4, :], gw[:, 2:4, :], gw[:, 0:2, :], ALU.add))
        link(dve.tensor_scalar(gT[:, 0:2, :], gw[:, 0:2, :], -1.0, None, ALU.mult))
        sync()
        dve.sem_inc(g_rows, 1)
        mean_k(0)
        norm_k(0)
        dve.wait_ge(g_colT, 1)
        dve.tensor_copy(gcol[:, :, :, :, :].rearrange("p w d t h -> p (w d t h)"), ps[:, 0, 0:64]
                        ).then_inc(g_cols, 1)
        qk_lo(0)
        v_lo(0)
        dve.wait_ge(g_stored, 16)
        looped(0, PAIRS - 1, 23, lambda p: pair(p, True))
        pair(PAIRS - 1, False)

        def head_weights(h):
            done = 0
            for t in range(TT):
                wf = (t + 1) * P
                done += (1 if t == 0 else 2) + (1 if t == TT - 1 else 2)
                dve.wait_ge(m_exp, 14 * h + done)
                dve.wait_ge(m_QK, TT * h + t + 1)
                if t == 0 and not (isinstance(h, int) and h == 0):
                    dve.wait_ge(m_WT, TT * h)
                dve.tensor_tensor_reduce(sf[:, t, 0:wf], ps[:, t, 0:wf], et[:, t % 2, 0:wf], DM ** -0.5, 0.0,
                                         ALU.mult, ALU.add, mden[:, 0, t:t + 1]).then_inc(m_S, 1)
                dve.tensor_tensor_reduce(sbw[:, t, t * P:S], ps[:, t, t * P:S], et[:, t % 2, wf:wf + S - t * P],
                                         DM ** -0.5, 0.0, ALU.mult, ALU.add, mden[:, 1, t:t + 1]
                                         ).then_inc(m_S, 1)
            dve.wait_ge(m_S, 2 * TT * (h + 1))
            link(dve.scalar_tensor_tensor(mden2[:, :, :], mden[:, :, :], -1.0, mden[:, :, :],
                                          ALU.mult, ALU.max))
            sync()
            link(dve.tensor_tensor(mden2[:, :, :], mden2[:, :, :],
                                   gcol[:, 1, :, :, bass.ds(h, 1)].rearrange("p d t a -> p d (t a)"), ALU.max))
            sync()
            dve.reciprocal(mrd[:, :, :], mden2[:, :, :]).then_inc(m_rd, 1)

        def head_diag(h):
            sc = 0
            for t in range(TT):
                sc += 2 if t < TT - 1 else 1
                dve.wait_ge(m_sc, 7 * h + sc)
                dg = slice(t * P, (t + 1) * P)
                dve.scalar_tensor_tensor(sf[:, t, dg], sbw[:, t, dg], mrd[:, 1, t:t + 1], sf[:, t, dg],
                                         ALU.mult, ALU.add).then_inc(m_w, 1)

        def head(h, nxt):
            for i, t in enumerate(WT_ORDER):
                q = slice(t * P, (t + 1) * P)
                dve.wait_ge(m_WThi, TT * h + i + 1)
                dve.tensor_tensor(wT[1][:, :, q], ps[:, 4 + t, :].rearrange("p (j n) -> p j n", j=TT),
                                  wT[0][:, :, q].bitcast(F), ALU.subtract).then_inc(m_WTlo, 1)
            if nxt:
                head_weights(h + 1)
            norm_mean(dve, nm, 6, DM, h)
            norm_diag(dve, nm, msq[:, 0, :], h)
            if nxt:
                head_diag(h + 1)
            dve.wait_ge(nm[5], h + 1)
            for v in range(2):
                dve.scalar_tensor_tensor(mt[:, v, :], ps[:, 4 + v, :], col(VT, V_MG + 2 * h + v),
                                         msq[:, 1, :], ALU.mult, ALU.mult).then_inc(m_normed, 1)
            dve.wait_ge(m_normed, 2 * h + 2)
            dve.wait_ge(m_v_in, 48 * (h + 1))
            for v in range(2):
                dve.tensor_tensor(mt[:, v, :], mt[:, v, :], mo[:, v, :], ALU.mult).then_inc(m_t2, 1)
            for v in range(2):
                dve.wait_ge(m_ohi, 2 * h + v + 1)
                to = mixM[:, bass.ds(2 * h + v, 1), :, :].rearrange("p a b n -> p (a b) n")
                dve.tensor_tensor(to[:, 1, :], mt[:, v, :], to[:, 0, :].bitcast(F),
                                  ALU.subtract).then_inc(m_olo, 1)
        head_weights(0)
        head_diag(0)
        for s in range(2):
            dve.wait_ge(mix_stored[s], 16 * PAIRS)
        looped(0, HM - 1, 2, lambda h: head(h, True))
        head(HM - 1, False)

        dve.wait_ge(ada_read, 16)

        def residual(gp, half):
            g = 2 * gp + half
            units = lambda us: ada_units(8 + g, us, araw2, acc2[:, 2 * half:2 * half + 2, :], False)
            units(range(4))
            if not (isinstance(g, int) and g == 0):
                m = M_G1 + 8 * (3 + g)
                ada_cols(7 + g, 4 * (1 - half) + 3, m, m + 4)
            units(range(4, 8))
            if isinstance(g, int) and g == 0:
                dve.wait_ge(xT_back, 16)
            dve.wait_ge(blk_done, N_OUT + GB * g + GB)
            for i in range(4):
                T = 4 * g + i
                dve.scalar_tensor_tensor(one(x1T, T), ps[:, 4 * half + i, :], col(M, M_G1 + T), one(x1T, T),
                                         ALU.mult, ALU.add).then_inc(x1_done, 1)
            dve.wait_ge(x1_done, 4 * g + 4)
            dve.sem_inc(o_free[half], 4)
            for i in range(4):
                T = 4 * g + i
                dve.wait_ge(o_sq, T + 1)
                dve.wait_ge(o_sqadd, T + 1)
                dve.tensor_tensor(sqacc2[:, :], sqacc2[:, :], sq2[:, i % 2, :], ALU.add).then_inc(o_sqadd, 1)
        for half in range(2):
            dve.sem_inc(o_free[half], 4)
            dve.sem_inc(f_free[half], 4)
        dve.memset(sqacc2[:, :], 0.0).then_inc(sq_zero, 1)
        dve.wait_ge(sq_zero, 1)
        dve.sem_inc(o_sqadd, 1)
        residual(0, 0)
        residual(0, 1)
        with dve.Fori(1, G_OUT // 2) as gp:
            residual(gp, 0)
            residual(gp, 1)
        norm_mean(dve, n2, 0, D)
        norm_diag(dve, n2, utmp2[:, 1, :])
        ada_cols(11, 3, M_G1 + 56, M_G1 + 60)
        dve.wait_ge(ada_read, 24)
        link(dve.scalar_tensor_tensor(A1[:, :], M[:, M_SC2:M_SC2 + KT], 1.0, VT[:, V_GMLP:V_GMLP + KT],
                                      ALU.add, ALU.mult))
        dve.wait_ge(n2[5], 1)
        sync()
        def h2_low(j):
            dve.wait_ge(h2_hi, j + 1)
            dve.scalar_tensor_tensor(h2T[1][:, j, :], utmp2[:, j % 2, :], M[:, M_SH2 + j:M_SH2 + j + 1],
                                     h2T[0][:, j, :].bitcast(F), ALU.add, ALU.subtract).then_inc(h2_lo, 1)
        modulate(range(KT), x1T, A1, rstd2, utmp2, u2_done, h2_lo, h2_low)

        dve.sem_inc(f_sq, 1)
        dve.sem_inc(f_lo, 1)
        with dve.Fori(0, CHUNKS) as ch:
            for q in range(2):
                T0 = CT * ch + 4 * q
                for i in range(5):
                    if i < 4:
                        dve.wait_ge(f_relu, T0 + i + 1)
                        dve.wait_ge(f_lo, T0 + max(i - 1, 0) + 1)
                        dve.tensor_tensor(sq2[:, i % 2, :], utmp2[:, i % 2, :], utmp2[:, i % 2, :], ALU.mult
                                          ).then_inc(f_sq, 1)
                    if i >= 1:
                        dve.wait_ge(f_hi, T0 + i)
                        dve.tensor_tensor(aT[1][:, 4 * q + i - 1, :], sq2[:, (i - 1) % 2, :],
                                          aT[0][:, 4 * q + i - 1, :].bitcast(F), ALU.subtract
                                          ).then_inc(f_lo, 1)
                dve.sem_inc(f_free[q], 4)
            for q in range(4):
                dve.wait_ge(blk_done, N_FF + CB * ch + 2 * GB + 4 * q + 4)
                for i in range(4):
                    T = 4 * q + i
                    dve.scalar_tensor_tensor(x1T[:, T, :], ps[:, 4 * (q % 2) + i, :],
                                             M[:, M_G2 + T:M_G2 + T + 1], x1T[:, T, :], ALU.mult, ALU.add
                                             ).then_inc(f_free[q % 2], 1)
        for t in range(TT):
            if t >= 2:
                dve.wait_ge(y_stored[t % 2], 16)
            for k in range(1, 4, 2):
                dve.wait_ge(y_T, 4 * t + k + 1)
                dve.tensor_copy(yst[:, t % 2, 512 * k:512 * k + 512], ps[:, 4 * (t % 2) + k, :]
                                ).then_inc(y_dve, 1)

    perm.close()


_INS = ["x", "c", "positions", "w_ada", "b_ada", "norm_mix_g", "w_in", "b_gates", "conv_w", "conv_b",
        "q_lora_g", "w_uq", "kv_lora_g", "w_ukv", "q_norm_g", "k_norm_g", "mlstm_norm_g",
        "w_out", "norm_mlp_g", "w_ff1", "w_ff2"]
_FLAT = {"w_ada": 2, "w_in": 2, "w_uq": 2, "w_ukv": 2, "w_out": 2, "w_ff1": 2, "w_ff2": 2, "x": 2}


def program(nc, shapes):
    aps = []
    for name in _INS:
        shape, dt = shapes[name]
        ap = nc.dram_tensor(f"in_{name}", shape, dt, kind="ExternalInput").ap()
        if name in _FLAT:
            ap = ap.rearrange("a m n -> (a m) n")
        elif len(shape) == 3:
            ap = ap.rearrange("a m n -> (a m n)")
        else:
            ap = ap.rearrange("a n -> (a n)")
        aps.append(ap)
    out = nc.dram_tensor("out", (1, S, D), F, kind="ExternalOutput").ap()
    build(nc, *aps, out.rearrange("a s d -> (a s) d"))


def kernel(**inputs):
    import concourse.bacc as bacc
    from concourse.bass_utils import run_bass_kernel_spmd

    nc = bacc.Bacc("TRN2", target_bir_lowering=False, num_devices=1)
    arrays = {f"in_{n}": np.ascontiguousarray(inputs[n]) for n in _INS}
    program(nc, {n: (arrays[f"in_{n}"].shape, mybir.dt.from_np(arrays[f"in_{n}"].dtype)) for n in _INS})
    r = run_bass_kernel_spmd(nc, [arrays], core_ids=[0])
    return r.results[0]["out"]
```
